# Optimizing a Trainium2 kernel written in Bass

```python
import jax, jax.numpy as jnp
from jax import lax
import numpy as np

D_MODEL = 1024
BATCH = 1
SEQ = 512
DEPTH = 1
DEC_BATCH = 8
DEC_SEQ = 8
PAST_LEN = 4096
PAGE_SIZE = 128

C_CONV = D_MODEL // 2
C_GMLP = D_MODEL - C_CONV
GMLP_HEADS = 8
GMLP_HEAD_DIM = C_GMLP // GMLP_HEADS
CONV_WIDTH = 31
CHUNK = 128
PLE_DIM = 256
N_GROUPS = 4
EXPERTS_PER_GROUP = 4
N_EXPERTS = N_GROUPS * EXPERTS_PER_GROUP
TOP_K = 2
D_EXPERT = D_MODEL // 2
D_IN = 2 * C_CONV + 2 * C_GMLP
EPS = 1e-6

kernel_name = "hymba_conv_gmlp_hmoe_step"

def rms_norm(x, g):
    xf = x.astype(jnp.float32)
    y = xf * lax.rsqrt(jnp.mean(xf * xf, axis=-1, keepdims=True) + EPS)
    return (y * g.astype(jnp.float32)).astype(x.dtype)

def layer_norm(x, g, b):
    xf = x.astype(jnp.float32)
    mu = jnp.mean(xf, axis=-1, keepdims=True)
    xc = xf - mu
    var = jnp.mean(xc * xc, axis=-1, keepdims=True)
    y = xc * lax.rsqrt(var + EPS) * g.astype(jnp.float32) + b.astype(jnp.float32)
    return y.astype(x.dtype)

def causal_depthwise_conv(buf, x, w, bias):
    xs = jnp.concatenate([buf, x], axis=1)
    y = lax.conv_general_dilated(
        xs, w[:, None, :], window_strides=(1,), padding='VALID',
        dimension_numbers=('NWC', 'WIO', 'NWC'), feature_group_count=xs.shape[-1])
    return y + bias, xs[:, -(CONV_WIDTH - 1):]

def chunk_spatial_mix(v, w_s, b_s, chunk_len):
    n, t, c = v.shape
    nc = t // chunk_len
    vh = v.reshape(n, nc, chunk_len, GMLP_HEADS, GMLP_HEAD_DIM)
    mask = jnp.tril(jnp.ones((chunk_len, chunk_len), dtype=bool))
    ws = jnp.where(mask[None], w_s[:, :chunk_len, :chunk_len], 0)
    mixed = jnp.einsum('hij,ncjhd->ncihd', ws, vh)
    mixed = mixed + jnp.transpose(b_s[:, :chunk_len])[None, None, :, :, None]
    return mixed.reshape(n, t, c)

def token_mixers(a, buf, chunk_len, w_in, conv_w, conv_b, conv_ln_g, conv_ln_b,
                 gmlp_ln_g, gmlp_ln_b, w_s, b_s, w_out):
    z = a @ w_in
    a_val, a_gate, b_u, b_v = jnp.split(
        z, [C_CONV, 2 * C_CONV, 2 * C_CONV + C_GMLP], axis=-1)
    glu = a_val * jax.nn.sigmoid(a_gate)
    conv_out, new_buf = causal_depthwise_conv(buf, glu, conv_w, conv_b)
    ya = jax.nn.silu(layer_norm(conv_out, conv_ln_g, conv_ln_b))
    u = jax.nn.gelu(b_u)
    v = layer_norm(jax.nn.gelu(b_v), gmlp_ln_g, gmlp_ln_b)
    yb = u * chunk_spatial_mix(v, w_s, b_s, chunk_len)
    out = jnp.concatenate([ya, yb], axis=-1) @ w_out
    return out, new_buf, v

def hierarchical_moe(c, w_rg, b_rg, w_re, b_re, w_gate, w_up, w_down):
    n, t, d = c.shape
    xf = c.reshape(n * t, d)
    gl = (xf @ w_rg + b_rg).astype(jnp.float32)
    gp = jax.nn.softmax(gl, axis=-1)
    g = jnp.argmax(gl, axis=-1)
    g_w = jnp.take_along_axis(gp, g[:, None], axis=1)
    el = (xf @ w_re + b_re).astype(jnp.float32).reshape(-1, N_GROUPS, EXPERTS_PER_GROUP)
    el_g = jnp.take_along_axis(el, g[:, None, None], axis=1)[:, 0]
    top_v, top_i = lax.top_k(el_g, TOP_K)
    w = jax.nn.softmax(top_v, axis=-1) * g_w
    ids = g[:, None] * EXPERTS_PER_GROUP + top_i
    combine = jnp.sum(jax.nn.one_hot(ids, N_EXPERTS, dtype=jnp.float32) * w[..., None], axis=1)
    y = jnp.zeros(xf.shape, jnp.float32)
    for e in range(N_EXPERTS):
        h = jax.nn.silu(xf @ w_gate[e]) * (xf @ w_up[e])
        y = y + combine[:, e:e + 1] * (h @ w_down[e]).astype(jnp.float32)
    return y.astype(c.dtype).reshape(n, t, d)

def decoder_layer(x, p, buf, chunk_len, norm_mix_g, w_in, conv_w, conv_b, conv_ln_g,
                  conv_ln_b, gmlp_ln_g, gmlp_ln_b, w_s, b_s, w_out, norm_ffn_g,
                  w_router_group, b_router_group, w_router_expert, b_router_expert,
                  w_exp_gate, w_exp_up, w_exp_down, norm_ple_g, w_ple_gate, w_ple_proj):
    mix, new_buf, v = token_mixers(rms_norm(x, norm_mix_g), buf, chunk_len, w_in, conv_w,
                                   conv_b, conv_ln_g, conv_ln_b, gmlp_ln_g, gmlp_ln_b,
                                   w_s, b_s, w_out)
    h = x + mix
    h = h + hierarchical_moe(rms_norm(h, norm_ffn_g), w_router_group, b_router_group,
                             w_router_expert, b_router_expert, w_exp_gate, w_exp_up,
                             w_exp_down)
    gate = jax.nn.sigmoid(rms_norm(h, norm_ple_g) @ w_ple_gate)
    h = h + (p @ w_ple_proj) * gate
    return h, new_buf, v

def setup_inputs(seed: int = 0) -> dict:
    key = jax.random.key(seed)
    ks = jax.random.split(key, 32)
    f32 = jnp.float32

    def nrm(k, shape, scale):
        return jax.random.normal(k, shape, f32) * scale

    def gain(k, shape):
        return 1.0 + 0.05 * jax.random.normal(k, shape, f32)

    return {
        "x_prompt": nrm(ks[0], (BATCH, SEQ, D_MODEL), 1.0),
        "x_sample": nrm(ks[1], (DEC_BATCH, DEC_SEQ, D_MODEL), 1.0),
        "p_prompt": nrm(ks[2], (DEPTH, BATCH, SEQ, PLE_DIM), 1.0),
        "p_sample": nrm(ks[3], (DEPTH, DEC_BATCH, DEC_SEQ, PLE_DIM), 1.0),
        "state_conv": nrm(ks[4], (DEPTH, DEC_BATCH, CONV_WIDTH - 1, C_CONV), 0.5),
        "norm_mix_g": gain(ks[5], (DEPTH, D_MODEL)),
        "w_in": nrm(ks[6], (DEPTH, D_MODEL, D_IN), D_MODEL ** -0.5),
        "conv_w": nrm(ks[7], (DEPTH, CONV_WIDTH, C_CONV), CONV_WIDTH ** -0.5),
        "conv_b": nrm(ks[8], (DEPTH, C_CONV), 0.02),
        "conv_ln_g": gain(ks[9], (DEPTH, C_CONV)),
        "conv_ln_b": nrm(ks[10], (DEPTH, C_CONV), 0.02),
        "gmlp_ln_g": gain(ks[11], (DEPTH, C_GMLP)),
        "gmlp_ln_b": nrm(ks[12], (DEPTH, C_GMLP), 0.02),
        "w_s": nrm(ks[13], (DEPTH, GMLP_HEADS, CHUNK, CHUNK), CHUNK ** -0.5),
        "b_s": gain(ks[14], (DEPTH, GMLP_HEADS, CHUNK)),
        "w_out": nrm(ks[15], (DEPTH, C_CONV + C_GMLP, D_MODEL), (C_CONV + C_GMLP) ** -0.5),
        "norm_ffn_g": gain(ks[16], (DEPTH, D_MODEL)),
        "w_router_group": nrm(ks[17], (DEPTH, D_MODEL, N_GROUPS), D_MODEL ** -0.5),
        "b_router_group": nrm(ks[18], (DEPTH, N_GROUPS), 0.01),
        "w_router_expert": nrm(ks[19], (DEPTH, D_MODEL, N_EXPERTS), D_MODEL ** -0.5),
        "b_router_expert": nrm(ks[20], (DEPTH, N_EXPERTS), 0.01),
        "w_exp_gate": nrm(ks[21], (DEPTH, N_EXPERTS, D_MODEL, D_EXPERT), D_MODEL ** -0.5),
        "w_exp_up": nrm(ks[22], (DEPTH, N_EXPERTS, D_MODEL, D_EXPERT), D_MODEL ** -0.5),
        "w_exp_down": nrm(ks[23], (DEPTH, N_EXPERTS, D_EXPERT, D_MODEL), D_EXPERT ** -0.5),
        "norm_ple_g": gain(ks[24], (DEPTH, D_MODEL)),
        "w_ple_gate": nrm(ks[25], (DEPTH, D_MODEL, D_MODEL), D_MODEL ** -0.5),
        "w_ple_proj": nrm(ks[26], (DEPTH, PLE_DIM, D_MODEL), PLE_DIM ** -0.5),
        "norm_final_g": gain(ks[27], (D_MODEL,)),
    }

def reference(x_prompt, x_sample, p_prompt, p_sample, state_conv, norm_mix_g, w_in, conv_w,
              conv_b, conv_ln_g, conv_ln_b, gmlp_ln_g, gmlp_ln_b, w_s, b_s, w_out,
              norm_ffn_g, w_router_group, b_router_group, w_router_expert, b_router_expert,
              w_exp_gate, w_exp_up, w_exp_down, norm_ple_g, w_ple_gate, w_ple_proj,
              norm_final_g):
    hp = x_prompt
    hs = x_sample
    dec_seq = x_sample.shape[1]
    conv_p_list, conv_s_list, v_s_list = [], [], []
    for i in range(DEPTH):
        lw = (norm_mix_g[i], w_in[i], conv_w[i], conv_b[i], conv_ln_g[i], conv_ln_b[i],
              gmlp_ln_g[i], gmlp_ln_b[i], w_s[i], b_s[i], w_out[i], norm_ffn_g[i],
              w_router_group[i], b_router_group[i], w_router_expert[i], b_router_expert[i],
              w_exp_gate[i], w_exp_up[i], w_exp_down[i], norm_ple_g[i], w_ple_gate[i],
              w_ple_proj[i])
        zero_buf = jnp.zeros((hp.shape[0], CONV_WIDTH - 1, C_CONV), hp.dtype)
        hp, conv_p, _ = decoder_layer(hp, p_prompt[i], zero_buf, CHUNK, *lw)
        hs, conv_s, v_s = decoder_layer(hs, p_sample[i], state_conv[i], dec_seq, *lw)
        conv_p_list.append(conv_p)
        conv_s_list.append(conv_s)
        v_s_list.append(v_s)
    y_prompt = rms_norm(hp, norm_final_g)
    y_sample = rms_norm(hs, norm_final_g)
    state_conv_prompt = jnp.stack(conv_p_list, axis=0)
    state_conv_sample = jnp.stack(conv_s_list, axis=0)
    state_gmlp_v_sample = jnp.stack(v_s_list, axis=0)
    return (y_prompt, y_sample, state_conv_prompt, state_conv_sample, state_gmlp_v_sample)


_drawn_inputs = setup_inputs


def setup_inputs(seed=0):
    import zlib

    import numpy as np

    out = dict(_drawn_inputs(seed))
    spreads = {}
    factors = {'conv_b': 2.714,
     'gmlp_ln_b': 2.881,
     'b_router_group': 3.124,
     'b_router_expert': 5.25,
     'norm_ple_g': 7.131,
     'conv_ln_b': 4.209}
    for name, (base, spread) in spreads.items():
        noise = np.random.default_rng([zlib.crc32(name.encode()), seed]).standard_normal(out[name].shape)
        drawn = base * np.exp(spread * noise) if base else spread * noise
        out[name] = __import__('jax').numpy.asarray(drawn.astype(out[name].dtype))
    for name, factor in factors.items():
        out[name] = (out[name] * factor).astype(out[name].dtype)
    return out
```

```python
from contextlib import ExitStack

import concourse.bass as bass
from concourse import mybir

F32 = mybir.dt.float32
F32R = mybir.dt.float32r
U32 = mybir.dt.uint32
ALU = mybir.AluOpType
ACT = mybir.ActivationFunctionType
AX_X = mybir.AxisListType.X

P = 128
D = 1024
SEQ = 512
DEC_BATCH = 8
DEC_SEQ = 8
SAMPLE = DEC_BATCH * DEC_SEQ
TOKENS = SEQ + SAMPLE
TILES = 5
HALF = TOKENS // 2
C = 512
CB = C // P
DC = D // P
HEADS = 8
HD = C // HEADS
WIDTH = 31
HIST = WIDTH - 1
GP = HIST + SEQ
GS = HIST + DEC_SEQ
GROW = GP + DEC_BATCH * GS
PLE = 256
GROUPS = 4
PER = 4
EXPERTS = GROUPS * PER
DE = D // 2
EPS = 1e-6
UNIT = 2048
UC = UNIT // DC
RAW = 6
SPLIT = 3
CAP = TILES * P
NOBODY = 4096
OVERFLOW_MAX = 8
BIG = 3.0e38

Z_COLS = [0, C, UC, C + UC, 3 * C, 3 * C + UC, 2 * C, 2 * C + UC]
N_OUT = len(Z_COLS)
N_PROJ = N_OUT + D // UC
N_MOE = N_PROJ + 1
N_STEP = N_MOE + 4
N_GATE = N_STEP + 6 * (EXPERTS - 1) + 2
N_UNITS = N_GATE + D // UC
N_CONST = 15 + 2 * TILES + 0
N_CONST_SQ = 3
LOW_POOL = 512
WORD_COLS = 2 * EXPERTS * CAP // P
MIX, FFN, GATE, FINAL = range(4)


def rows(t):
    return P if t < TILES - 1 else SAMPLE


def hybrid_layer(nc, a, out):
    ctx = ExitStack()

    def sb(name, shape, dt=F32):
        return ctx.enter_context(nc.sbuf_tensor(name, shape, dt))

    def sem(name):
        return ctx.enter_context(nc.semaphore(name))

    with ctx:
        raw = sb("raw", [P, RAW, UNIT])
        hi = sb("hi", [P, SPLIT, UNIT], F32R)
        lo = sb("lo", [P, SPLIT, UNIT], F32R)
        act_hi = sb("act_hi", [P, DC * TOKENS], F32R)
        act_lo = sb("act_lo", [P, DC * TOKENS], F32R)
        h = sb("h", [P, TILES * D])
        conv = sb("conv", [P, CB * (GROW + TOKENS)])
        ws = sb("ws", [P, HEADS * (P + SAMPLE)])
        wide = sb("wide", [P, D])
        two = sb("two", [P, 2 * D])
        work = sb("work", [P, D])
        gain = sb("gain", [P, D])
        ident = sb("ident", [P, P])
        before = sb("before", [P, P])
        ones = sb("ones", [P, P])
        vecs = sb("vecs", [P, CB, WIDTH + 3])
        wr = sb("wr", [P, DC, GROUPS + EXPERTS])
        rb = sb("rb", [P, GROUPS + EXPERTS])
        sq = sb("sq", [P, 4, 8])
        rs = sb("rs", [P, 4, 8])
        st = sb("st", [P, 2, TILES, 8])
        mv = sb("mv", [P, 2, TILES, 2])
        lr = sb("lr", [P, 2, 8])
        lg = sb("lg", [P, TILES, GROUPS + EXPERTS])
        r1 = sb("r1", [P, 16, TILES])
        rev = sb("rev", [P, GROUPS])
        base = sb("base", [P, EXPERTS])
        pos = sb("pos", [P, TILES, 2], U32)
        pays = sb("pays", [P, TILES, 2, 2], U32)
        lists = sb("lists", [P, EXPERTS, 2], U32)
        gidx = sb("gidx", [P, 1], U32)
        sidx = sb("sidx", [P, 1], U32)
        token = sb("token", [1, 3])
        oidx = sb("oidx", [P, 2], U32)
        wl = sb("wl", [1, 3, 4 * EXPERTS])
        codes = sb("codes", [1, 2, 4 * EXPERTS])
        jobs = sb("jobs", [1, 2 * OVERFLOW_MAX + 1])
        jobs_i = sb("jobs_i", [1, 2 * OVERFLOW_MAX + 1], U32)
        pair = [ctx.enter_context(nc.psum_tensor(f"pair{i}", [P, 2 * 512], F32)) for i in range(4)]
        bank = [pair[i // 2][:, i % 2 * 512:(i % 2 + 1) * 512] for i in range(8)]

        normed = nc.dram_tensor("normed", (TOKENS, D), F32, kind="Internal").ap()
        pairs = nc.dram_tensor("pairs", (2 * TOKENS, D), F32, kind="Internal").ap()
        slots = nc.dram_tensor("slots", (EXPERTS * CAP, 2), U32, kind="Internal").ap()

        H = h[:, :].rearrange("p (t d) -> p t d", t=TILES)
        V = h[:, 0:TILES * C].rearrange("p (t c) -> p t c", t=TILES)
        U = h[:, TILES * C:TILES * C + CB * TOKENS].rearrange("p (b n) -> p b n", b=CB)
        G = conv[:, 0:CB * GROW].rearrange("p (b n) -> p b n", b=CB)
        A = conv[:, CB * GROW:].rearrange("p (b n) -> p b n", b=CB)
        PP = conv[:, 0:TILES * D].rearrange("p (t d) -> p t d", t=TILES)
        GSAM = G[:, :, GP:].rearrange("p b (s k) -> p b s k", s=DEC_BATCH)
        WS = ws[:, 0:HEADS * P].rearrange("p (h n) -> p h n", h=HEADS)
        WSS = ws[:, HEADS * P:].rearrange("p (h n) -> p h n", h=HEADS)
        PN = ws[:, 0:TILES * PLE].rearrange("p (t d) -> p t d", t=TILES)
        ahi = act_hi[:, :].rearrange("p (c n) -> p c n", c=DC)
        alo = act_lo[:, :].rearrange("p (c n) -> p c n", c=DC)
        X_AT, HT_AT, P_AT = 0, DC * P, DC * P + CB * P
        xhi, xlo = (s[:, X_AT:HT_AT].rearrange("p (c n) -> p c n", c=DC) for s in (act_hi, act_lo))
        thi, tlo = (s[:, HT_AT:P_AT].rearrange("p (c n) -> p c n", c=CB) for s in (act_hi, act_lo))
        phi, plo = (s[:, P_AT:P_AT + 2 * TOKENS].rearrange("p (c n) -> p c n", c=2) for s in (act_hi, act_lo))
        xg = two[:, 0:D]
        res = two[:, D:2 * D]
        stn = two[:, 0:2 * C].rearrange("p (i c) -> p i c", i=2)
        SROWS = DEC_BATCH * HIST // 2
        vrow = two[:, 2 * C:3 * C]
        NV = WIDTH + 3
        wssn = two[:, 3 * C:4 * C].rearrange("p (h n) -> p h n", h=HEADS)
        wsn = wide[:, :].rearrange("p (h n) -> p h n", h=HEADS)
        lng, lnb = work[:, 0:C], work[:, C:2 * C]
        sg = gain[:, 0:TOKENS]
        fresh = gain[:, TOKENS:TOKENS + CB * SAMPLE].rearrange("p (b n) -> p b n", b=CB)
        silu, hid = work[:, 0:DE], work[:, DE:2 * DE]
        BS = 64
        bs = two[BS:BS + 1, D:2 * D]
        r16 = conv[:, TILES * D:TILES * D + 6 * TILES * EXPERTS].rearrange("p (a t e) -> p a t e", a=6, t=TILES)
        r4 = ws[:, TILES * PLE:TILES * (PLE + 8 * GROUPS)].rearrange("p (a t g) -> p a t g", a=8, t=TILES)
        wl8 = wide[0:1, :].rearrange("p (q j n) -> p q j n", q=2, j=OVERFLOW_MAX)
        empty = conv[:, TILES * D:TILES * D + WORD_COLS].bitcast(U32)

        x_in = [sem(f"x_in{t}") for t in range(TILES)]
        gain_in = sem("gain_in")
        ln_in = sem("ln_in")
        ws_in = sem("ws_in")
        rows_in = sem("rows_in")
        small_in = sem("small_in")
        raw_in = [sem(f"raw_in{i}") for i in range(RAW)]
        hi_done = sem("hi_done")
        lo_pool = sem("lo_pool")
        lo_dve = sem("lo_dve")
        pe_unit = sem("pe_unit")
        const = sem("const")
        sq_done = sem("sq_done")
        mean_done = sem("mean_done")
        root_done = sem("root_done")
        norm_done = sem("norm_done")
        xt_ps = sem("xt_ps")
        xt_hi = sem("xt_hi")
        xt_lo = sem("xt_lo")
        setup_ps = sem("setup_ps")
        setup_sb = sem("setup_sb")
        masked = sem("masked")
        z_ps = sem("z_ps")
        sig_done = sem("sig_done")
        glu_done = sem("glu_done")
        acc_p = sem("acc_p")
        acc_s = sem("acc_s")
        v_ps = sem("v_ps")
        v_gelu = sem("v_gelu")
        u_ps = sem("u_ps")
        u_gelu = sem("u_gelu")
        v_norm = sem("v_norm")
        v_scaled = sem("v_scaled")
        v_ready = sem("v_ready")
        var_done = sem("var_done")
        sd_done = sem("sd_done")
        ct_ps = sem("ct_ps")
        ct_norm = sem("ct_norm")
        cc_ps = sem("cc_ps")
        ya_silu = sem("ya_silu")
        ya_hi = sem("ya_hi")
        ya_lo = sem("ya_lo")
        mix_ps = sem("mix_ps")
        yb_mul = sem("yb_mul")
        yb_hi = sem("yb_hi")
        yb_lo = sem("yb_lo")
        x_again = sem("x_again")
        fresh_done = sem("fresh_done")
        state_ps = sem("state_ps")
        state_sb = sem("state_sb")
        o_ps = sem("o_ps")
        o_add = sem("o_add")
        normed_out = [sem(f"normed_out{i}") for i in range(2)]
        rt_ps = sem("rt_ps")
        rt_sb = sem("rt_sb")
        r_ps = sem("r_ps")
        lg_sb = sem("lg_sb")
        p_in = sem("p_in")
        pt_ps = sem("pt_ps")
        pt_hi = sem("pt_hi")
        pt_lo = sem("pt_lo")
        pp_ps = sem("pp_ps")
        pp_sb = sem("pp_sb")
        arg_done = sem("arg_done")
        exp_done = sem("exp_done")
        onehot = sem("onehot")
        rank_ps = sem("rank_ps")
        slot_at = sem("slot_at")
        slots_clear = sem("slots_clear")
        filler_set = sem("filler_set")
        slots_out = sem("slots_out")
        lists_in = sem("lists_in")
        gidx_set = sem("gidx_set")
        sidx_set = sem("sidx_set")
        gathered = sem("gathered")
        g_ps = sem("g_ps")
        g_hi = sem("g_hi")
        g_lo = sem("g_lo")
        silu_done = sem("silu_done")
        hid_done = sem("hid_done")
        t_ps = sem("t_ps")
        t_hi = sem("t_hi")
        t_lo = sem("t_lo")
        res_act = sem("res_act")
        res_dve = sem("res_dve")
        scattered = sem("scattered")
        jobs_done = sem("jobs_done")
        v_idx = sem("v_idx")
        v_w = [sem(f"v_w{i}") for i in range(3)]
        v_in = sem("v_in")
        v_gps = sem("v_gps")
        v_gsb = sem("v_gsb")
        v_gu = sem("v_gu")
        v_silu = sem("v_silu")
        v_hid = sem("v_hid")
        v_tps = sem("v_tps")
        v_tsb = sem("v_tsb")
        v_dps = sem("v_dps")
        v_res = sem("v_res")
        v_out = sem("v_out")
        v_free = sem("v_free")
        pairs_full = sem("pairs_full")
        pair_in = sem("pair_in")
        pair_add = sem("pair_add")
        s_ps = sem("s_ps")
        s_sig = sem("s_sig")
        s_mul = sem("s_mul")
        s_add = sem("s_add")
        y_sb = sem("y_sb")
        y_out = [sem(f"y_out{i}") for i in range(2)]
        store = sem("store")
        dve = sem("dve")
        block = ctx.enter_context(nc.Block())

        def unit_source(n, d=0):
            def cols(w, at):
                return w[0, :, at:at + UC].rearrange("(c p) n -> p c n", p=P)
            if n < N_OUT:
                return cols(a["w_in"], Z_COLS[n])
            if n < N_PROJ:
                return cols(a["w_out"], (n - N_OUT) * UC)
            if n == N_PROJ:
                return a["w_ple_proj"][0].rearrange("(c p) n -> p c n", p=P)
            if n >= N_GATE:
                return cols(a["w_ple_gate"], (n - N_GATE) * UC)
            k, e = (n - N_MOE, 0) if n < N_STEP else ((n - N_STEP) % 6, 1 + (n - N_STEP) // 6)
            if n >= N_STEP + 6 * (EXPERTS - 1):
                k, e = 4 + (n - N_STEP - 6 * (EXPERTS - 1)), EXPERTS
            e = e + d
            if k < 4:
                w = a["w_exp_gate"] if k < 2 else a["w_exp_up"]
                w = w[0].rearrange("e (c p) n -> (e c) p n", p=P)
                at = e * DC + (k % 2) * (DC // 2)
                return w[bass.ds(at, DC // 2)].rearrange("c p n -> p c n")
            w = a["w_exp_down"][0].rearrange("e (c p) n -> (e c) p n", p=P)
            at = (e - 1) * CB + (k - 4) * 2
            return w[bass.ds(at, 2)].rearrange("c p n -> p c n")

        def wait_all(eng, *waits):
            waits = [(signal, value if isinstance(value, int) else eng.to_reg(value)) for signal, value in waits]
            eng.wait_ge(x_in[0], 16)
            for signal, value in waits:
                eng.wait_ge(signal, value)

        def used(n):
            if n < 4:
                return z_ps, 4 * (n // 2) + n % 2 + 3
            if n < 6:
                return v_ps, TILES * (n - 3)
            if n < N_OUT:
                return u_ps, 2 * (n - 5)
            if n < N_PROJ:
                return o_ps, TILES * (n - N_OUT + 1)
            if n == N_PROJ:
                return pp_ps, TILES
            if n < N_GATE:
                return pe_unit, n - N_MOE + 1
            return s_ps, TILES * (n - N_GATE + 1)

        def wait_used(eng, n, d=0):
            signal, value = used(n)
            eng.wait_ge(signal, value + 6 * d)

        def step_unit(e0, k):
            return N_STEP + 6 * (e0 - 1) + k

        @block.sync
        def _(sp):
            def load_unit(n, d=0):
                if n >= RAW:
                    done = n - RAW + 1 + 6 * d
                    low = [(lo_dve, n - RAW - N_MOE + 1 + 6 * d)] if N_MOE <= n - RAW < N_GATE else []
                    wait_all(sp, (hi_done, done), (lo_pool, done), *low)
                src = unit_source(n, d)
                sp.dma_start(raw[:, n % RAW, :].rearrange("p (c n) -> p c n", c=src.shape[1]), src)\
                  .then_inc(raw_in[n % RAW], 16)

            for t in range(TILES):
                x = a["x_prompt"][0, t * P:(t + 1) * P] if t < TILES - 1 else a["x_sample"].rearrange("b s d -> (b s) d")
                sp.dma_start(H[0:rows(t), t, :], x).then_inc(x_in[t], 16)
            for n in range(RAW):
                load_unit(n)
            sp.dma_start(out["state_conv_sample"][0, :, 0:HIST - DEC_SEQ],
                         a["state_conv"][0, :, DEC_SEQ:HIST]).then_inc(store, 16)
            for n in range(RAW, N_OUT):
                load_unit(n)
            for n in range(N_OUT, N_OUT + 3):
                load_unit(n)
            sp.wait_ge(v_ready, TILES)
            sp.dma_start(out["state_gmlp_v_sample"][0].rearrange("b s c -> (b s) c"),
                         V[0:SAMPLE, TILES - 1, :]).then_inc(store, 16)
            sp.wait_ge(yb_mul, TILES)
            sp.wait_ge(store, 32)
            for t in range(TILES):
                x = a["x_prompt"][0, t * P:(t + 1) * P] if t < TILES - 1 else a["x_sample"].rearrange("b s d -> (b s) d")
                sp.dma_start(H[0:rows(t), t, :], x).then_inc(x_again, 16)
            sp.wait_ge(state_sb, 1)
            sp.dma_start(out["state_conv_prompt"][0, 0], work[0:HIST, 0:C]).then_inc(store, 16)
            sp.wait_ge(state_sb, 2)
            for s in range(DEC_BATCH):
                sp.dma_start(out["state_conv_sample"][0, s, HIST - DEC_SEQ:HIST],
                             work[s * DEC_SEQ:(s + 1) * DEC_SEQ, C:2 * C]).then_inc(store, 16)
            for n in range(N_OUT + 3, N_STEP):
                load_unit(n)
            sp.wait_ge(slots_out, 16 * 2 * TILES)
            sp.dma_start(lists[:, :, :], slots.rearrange("(e s) k -> s e k", s=CAP)[0:P]).then_inc(lists_in, 16)
            for k in range(6):
                load_unit(step_unit(1, k))
            with sp.Fori(0, EXPERTS - 2) as d:
                for k in range(6):
                    load_unit(step_unit(2, k), d)
            for n in range(N_GATE - 2, N_GATE):
                load_unit(n)

            sp.wait_ge(jobs_done, 1)
            jobs_n = sp.value_load(jobs_i[0:1, 2 * OVERFLOW_MAX:], min_val=0, max_val=OVERFLOW_MAX)
            with sp.If(jobs_n > 0):
                sp.wait_ge(hi_done, N_GATE)
                sp.wait_ge(lo_pool, N_GATE)
                sp.wait_ge(lo_dve, N_GATE - N_MOE)
                with sp.Fori(0, jobs_n) as j:
                    e = sp.value_load(jobs_i[0:1, bass.ds(j, 1)], min_val=0, max_val=EXPERTS - 1)
                    at = sp.value_load(jobs_i[0:1, bass.ds(j + OVERFLOW_MAX, 1)], min_val=0, max_val=EXPERTS * CAP - P)
                    wait_all(sp, (v_free, j + 1))
                    sp.dma_start(oidx[:, :], slots[bass.ds(at, P), :]).then_inc(v_idx, 16)
                    for i, (w, c) in enumerate((("w_exp_gate", DC), ("w_exp_up", DC), ("w_exp_down", CB))):
                        src = a[w][0].rearrange("e (c p) n -> (e c) p n", p=P)
                        sp.dma_start(raw[:, 2 * i:2 * i + 2, :].rearrange("p s (c n) -> p (s c) n", c=c // 2),
                                     src[bass.ds(e * c, c)].rearrange("c p n -> p c n")).then_inc(v_w[i], 16)
            sp.wait_ge(pairs_full, 1)
            for n in range(N_GATE, N_UNITS):
                load_unit(n)
            for t in range(TILES):
                if t >= 1:
                    sp.wait_ge(pair_add, 2 * t)
                sp.dma_start(two[0:rows(t), :], pairs[2 * P * t:2 * (P * t + rows(t)), :].rearrange("(n k) d -> n (k d)", k=2))\
                  .then_inc(pair_in, 16)
            for t in range(TILES):
                sp.wait_ge(y_sb, t + 1)
                y = out["y_prompt"][0, t * P:(t + 1) * P] if t < TILES - 1 else out["y_sample"].rearrange("b s d -> (b s) d")
                sp.dma_start(y, two[0:rows(t), (t % 2) * D:(t % 2 + 1) * D]).then_inc(y_out[t % 2], 16)
            for i in range(2):
                sp.wait_ge(y_out[i], 16 * ((TILES + 1 - i) // 2))
            sp.wait_ge(store, 16 * (3 + DEC_BATCH))

        @block.gpsimd
        def _(g):
            own = [0]

            def made(ins):
                ins.then_inc(const, 1)
                own[0] += 1

            def link(ins):
                made(ins)
                g.wait_ge(const, own[0])

            def select(t, op, fill, start, pattern, mult):
                return nc.gpsimd.affine_select(out=t, in_=t, compare_op=op, fill=fill, base=start,
                                               pattern=pattern, channel_multiplier=mult)

            link(nc.gpsimd.memset(ident[:, :], 0.0))
            made(select(ident[:, :], ALU.not_equal, 1.0, 0, [[-1, P]], 1))
            made(nc.gpsimd.memset(sq[:, :, :], 1.0))
            made(nc.gpsimd.memset(G[:, :, 0:HIST], 0.0))
            made(nc.gpsimd.memset(mv[:, :, :, :], 1.0))
            made(nc.gpsimd.memset(ones[:, :], 1.0))
            link(nc.gpsimd.memset(wssn[0:SAMPLE], 0.0))
            for s in range(DEC_BATCH):
                r = slice(s * DEC_SEQ, (s + 1) * DEC_SEQ)
                nc.gpsimd.dma_start(wssn[r, :, r], a["w_s"][0, :, 0:DEC_SEQ, 0:DEC_SEQ].rearrange("h i j -> i h j"))\
                  .then_inc(ws_in, 16)
            nc.gpsimd.dma_start(wsn, a["w_s"][0].rearrange("h i j -> i h j")).then_inc(ws_in, 16)
            nc.gpsimd.memset(empty, NOBODY).then_inc(filler_set, 1)
            g.wait_ge(filler_set, 1)
            nc.gpsimd.dma_start(slots.rearrange("(p s) k -> p (s k)", p=P), empty).then_inc(slots_clear, 16)

            def split_low(n, d=0):
                share = LOW_POOL if N_MOE <= n < N_GATE else UNIT
                g.wait_ge(hi_done, n + 1 + 6 * d)
                if n >= SPLIT:
                    wait_used(g, n - SPLIT, d)
                s = slice(UNIT - share, UNIT)
                nc.gpsimd.tensor_tensor(lo[:, n % SPLIT, s], raw[:, n % RAW, s],
                                        hi[:, n % SPLIT, s].bitcast(F32), ALU.subtract).then_inc(lo_pool, 1)

            for n in range(SPLIT):
                split_low(n)
            g.wait_ge(ws_in, 16 * (DEC_BATCH + 1))
            select(wsn, ALU.is_ge, 0.0, 0, [[0, HEADS], [-1, P]], 1).then_inc(masked, 1)
            select(wssn[0:SAMPLE], ALU.is_ge, 0.0, 0, [[0, HEADS], [-1, SAMPLE]], 1).then_inc(masked, 1)
            link(nc.gpsimd.memset(before[:, :], 1.0))
            made(select(before[:, :], ALU.is_gt, 0.0, 0, [[1, P]], -1))
            made(nc.gpsimd.iota(rev[:, :], [[-1, GROUPS]], base=GROUPS, channel_multiplier=0,
                                allow_small_or_imprecise_dtypes=True))
            made(nc.gpsimd.iota(base[:, :], [[CAP, EXPERTS]], base=0, channel_multiplier=0,
                                allow_small_or_imprecise_dtypes=True))
            for t in range(TILES):
                made(nc.gpsimd.iota(pays[:, t, :, 0], [[0, 2]], base=P * t, channel_multiplier=1))
                made(nc.gpsimd.iota(pays[:, t, :, 1], [[1, 2]], base=2 * P * t, channel_multiplier=2))
            made(nc.gpsimd.iota(codes[:, 0, :], [[0, 4], [1, EXPERTS]], base=0, channel_multiplier=0,
                                allow_small_or_imprecise_dtypes=True))
            made(nc.gpsimd.iota(codes[:, 1, :], [[P, 4], [CAP, EXPERTS]], base=P, channel_multiplier=0,
                                allow_small_or_imprecise_dtypes=True))
            made(nc.gpsimd.memset(wl[:, 2, :], 0.0))
            made(nc.gpsimd.memset(lg[:, :, :], 0.0))
            assert own[0] == N_CONST
            for n in range(SPLIT, N_OUT):
                split_low(n)
            g.wait_ge(ln_in, 32)
            for t in range(TILES):
                r = rows(t)
                g.wait_ge(v_norm, t + 1)
                nc.gpsimd.tensor_tensor(V[0:r, t, :], V[0:r, t, :], lng[0:r], ALU.mult).then_inc(v_scaled, 1)
                g.wait_ge(v_scaled, t + 1)
                nc.gpsimd.tensor_tensor(V[0:r, t, :], V[0:r, t, :], lnb[0:r], ALU.add).then_inc(v_ready, 1)
            for n in range(N_OUT, N_MOE + 2):
                split_low(n)
            g.wait_ge(rt_ps, TILES)
            for i in range(2):
                g.wait_ge(normed_out[i], 16 * ((TILES + 1 - i) // 2))
            nc.gpsimd.memset(xg, 0.0).then_inc(gidx_set, 1)
            g.wait_ge(slots_clear, 16)
            g.wait_ge(slot_at, 1)
            for t in range(TILES):
                for k in range(2):
                    nc.gpsimd.indirect_dma_start(
                        slots, bass.IndirectOffsetOnAxis(pos[0:rows(t), t, k:k + 1], 0),
                        pays[0:rows(t), t, k, :], None).then_inc(slots_out, 16)

            last_token = g.to_reg(TOKENS - 1)
            last_pair = g.to_reg(2 * TOKENS - 1)

            def gather(e0, d=0):
                if e0 > 0:
                    g.wait_ge(gathered, 16 * (e0 + d))
                    g.wait_ge(g_ps, e0 + d)
                nc.gpsimd.tensor_copy(gidx[:, :], lists[:, bass.ds(e0 + d, 1), 0]).then_inc(gidx_set, 1)
                wait_all(g, (gidx_set, e0 + 2 + d))
                nc.gpsimd.indirect_dma_start(xg, None, normed, bass.IndirectOffsetOnAxis(gidx[:, :], 0),
                                             bounds_check=last_token, oob_is_err=False).then_inc(gathered, 16)

            def scatter(e0, d=0):
                if e0 > 0:
                    g.wait_ge(scattered, 16 * (e0 + d))
                nc.gpsimd.tensor_copy(sidx[:, :], lists[:, bass.ds(e0 + d, 1), 1]).then_inc(sidx_set, 1)
                wait_all(g, (sidx_set, e0 + 1 + d), (res_act, e0 + 1 + d), (res_dve, e0 + 1 + d))
                nc.gpsimd.indirect_dma_start(pairs, bass.IndirectOffsetOnAxis(sidx[:, :], 0), res, None,
                                             bounds_check=last_pair, oob_is_err=False).then_inc(scattered, 16)

            def step(e0, d=0):
                if e0 < EXPERTS - 1:
                    gather(e0 + 1, d)
                if e0 == 0:
                    for n in range(N_MOE + 2, N_STEP + 2):
                        split_low(n)
                    return
                for k in range(2, 8):
                    split_low(step_unit(e0, k), d)
                scatter(e0 - 1, d)

            g.wait_ge(lists_in, 16)
            g.wait_ge(gidx_set, 1)
            gather(0)
            step(0)
            step(1)
            with g.Fori(0, EXPERTS - 3) as d:
                step(2, d)
            for k in range(2, 8):
                split_low(step_unit(EXPERTS - 1, k))
            scatter(EXPERTS - 2)
            scatter(EXPERTS - 1)
            g.wait_ge(scattered, 16 * EXPERTS)
            nc.gpsimd.memset(token[:, 2:3], 0.0).then_inc(v_free, 1)

            g.wait_ge(jobs_done, 1)
            jobs_n = g.value_load(jobs_i[0:1, 2 * OVERFLOW_MAX:], min_val=0, max_val=OVERFLOW_MAX)
            with g.If(jobs_n > 0):
                with g.Fori(0, jobs_n) as j:
                    wait_all(g, (v_idx, 16 * j + 16))
                    nc.gpsimd.indirect_dma_start(xg, None, normed, bass.IndirectOffsetOnAxis(oidx[:, 0:1], 0),
                                                 bounds_check=last_token, oob_is_err=False).then_inc(v_in, 16)
                    wait_all(g, (v_res, j + 1))
                    nc.gpsimd.indirect_dma_start(pairs, bass.IndirectOffsetOnAxis(oidx[:, 1:2], 0), res, None,
                                                 bounds_check=last_pair, oob_is_err=False).then_inc(v_out, 16)
                    wait_all(g, (v_out, 16 * j + 16))
                    nc.gpsimd.memset(token[:, 0:1], 0.0).then_inc(v_free, 1)
            nc.gpsimd.memset(token[:, 1:2], 0.0).then_inc(pairs_full, 1)
            for n in range(N_GATE, N_UNITS):
                split_low(n)

        @block.scalar
        def _(act):
            def copy(out_, in_):
                return nc.scalar.activation(out_, in_, ACT.Copy)

            def load_gain(name):
                src = a[name] if len(a[name].shape) == 2 else a[name].rearrange("(o d) -> o d", o=1)
                act.dma_start(gain[:, :], src.to_broadcast([P, D])).then_inc(gain_in, 16)

            def split_high(n, d=0):
                act.wait_ge(raw_in[n % RAW], 16 * (n // RAW + 1) + 16 * d)
                if n >= SPLIT:
                    wait_used(act, n - SPLIT, d)
                copy(hi[:, n % SPLIT, :], raw[:, n % RAW, :]).then_inc(hi_done, 1)

            def square(t, w):
                nc.scalar.activation(work[0:rows(t), :], H[0:rows(t), t, :], ACT.Square,
                                     accum_out=sq[0:rows(t), w, t:t + 1]).then_inc(sq_done, 1)

            def root(w):
                act.wait_ge(mean_done, w + 1)
                nc.scalar.activation(rs[:, w, 0:TILES], rs[:, w, 0:TILES], ACT.Sqrt).then_inc(root_done, 1)

            def normed_high(t, w):
                r = rows(t)
                act.wait_ge(xt_ps, (0 if w == MIX else TILES) + t + 1)
                copy(ahi[:, :, t * P:t * P + r], pair[t % 2][:, :].rearrange("p (c n) -> p c n", c=DC)[:, :, 0:r])\
                    .then_inc(xt_hi, 1)

            act.dma_start(vrow[0:WIDTH, :], a["conv_w"][0]).then_inc(rows_in, 16)
            for i, name in enumerate(("conv_b", "conv_ln_g", "conv_ln_b")):
                act.dma_start(vrow[WIDTH + i:WIDTH + i + 1, :], a[name]).then_inc(rows_in, 16)
            states = a["state_conv"][0].rearrange("s k c -> (s k) c")
            for i in range(2):
                act.dma_start(stn[0:SROWS, i, :], states[i * SROWS:(i + 1) * SROWS]).then_inc(rows_in, 16)
            load_gain("norm_mix_g")
            act.dma_start(bs, a["b_s"].rearrange("o h n -> o (h n)")).then_inc(small_in, 16)
            act.dma_start(wr[:, :, 0:GROUPS], a["w_router_group"][0].rearrange("(c p) n -> p c n", p=P)).then_inc(small_in, 16)
            act.dma_start(wr[:, :, GROUPS:], a["w_router_expert"][0].rearrange("(c p) n -> p c n", p=P)).then_inc(small_in, 16)
            act.dma_start(rb[:, 0:GROUPS], a["b_router_group"].to_broadcast([P, GROUPS])).then_inc(small_in, 16)
            act.dma_start(rb[:, GROUPS:], a["b_router_expert"].to_broadcast([P, EXPERTS])).then_inc(small_in, 16)
            act.wait_ge(const, N_CONST_SQ)
            for t in range(TILES):
                act.wait_ge(x_in[t], 16)
                if t > 0:
                    act.wait_ge(sq_done, t)
                square(t, MIX)
            act.wait_ge(sq_done, TILES)
            act.dma_start(lng, a["gmlp_ln_g"].to_broadcast([P, C])).then_inc(ln_in, 16)
            act.dma_start(lnb, a["gmlp_ln_b"].to_broadcast([P, C])).then_inc(ln_in, 16)
            act.wait_ge(setup_ps, 1)
            copy(vecs[:, :, :], bank[4].rearrange("p (b n) -> p b n", b=CB)[:, :, 0:NV]).then_inc(setup_sb, 1)
            for i in range(2):
                act.wait_ge(setup_ps, 2 + i)
                for b in range(CB):
                    copy(GSAM[:, b, 4 * i:4 * i + 4, 0:HIST],
                         bank[5 + i][:, b * P:b * P + SROWS].rearrange("p (s k) -> p s k", k=HIST)).then_inc(setup_sb, 1)
            root(MIX)
            for n in range(SPLIT):
                split_high(n)
            for t in range(TILES):
                normed_high(t, MIX)

            def sigmoid(b):
                act.wait_ge(z_ps, 2 * b + 2)
                if b == 0:
                    act.wait_ge(norm_done, TILES)
                else:
                    act.wait_ge(glu_done, 3 * b)
                nc.scalar.activation(sg.rearrange("p (s n) -> p s n", s=2),
                                     pair[2 * (b % 2) + 1][:, :].rearrange("p (s n) -> p s n", s=2)[:, :, 0:HALF],
                                     ACT.Sigmoid).then_inc(sig_done, 1)

            for b in range(CB):
                sigmoid(b)
                split_high(SPLIT + b)
            for q in range(2 * TILES):
                i, t = divmod(q, TILES)
                act.wait_ge(v_ps, q + 1)
                nc.scalar.activation(V[0:rows(t), t, i * UC:(i + 1) * UC], bank[q % 4][0:rows(t), 0:UC],
                                     ACT.Gelu_apprx_tanh).then_inc(v_gelu, 1)
                if t == TILES - 1:
                    split_high(7 + i)
            act.wait_ge(var_done, 1)
            nc.scalar.activation(lr[:, 0, 0:TILES], lr[:, 0, 0:TILES], ACT.Sqrt).then_inc(sd_done, 1)
            for b in range(CB):
                act.wait_ge(u_ps, b + 1)
                nc.scalar.activation(U[:, b, :].rearrange("p (s n) -> p s n", s=2),
                                     pair[2 + b % 2][:, :].rearrange("p (s n) -> p s n", s=2)[:, :, 0:HALF],
                                     ACT.Gelu_apprx_tanh).then_inc(u_gelu, 1)
                if b % 2:
                    split_high(9 + b // 2)
            act.wait_ge(glu_done, 3 * CB)
            copy(fresh.rearrange("p b (s k) -> p b s k", k=DEC_SEQ), GSAM[:, :, :, HIST:]).then_inc(fresh_done, 1)
            act.wait_ge(setup_ps, 4)
            copy(WS, pair[0][:, :].rearrange("p (h n) -> p h n", h=HEADS)).then_inc(setup_sb, 1)
            act.wait_ge(setup_ps, 5)
            copy(WSS[0:SAMPLE], bank[2][0:SAMPLE, :].rearrange("p (h n) -> p h n", h=HEADS)).then_inc(setup_sb, 1)
            for t in range(TILES):
                act.wait_ge(yb_mul, t + 1)
                copy(ahi[:, CB:, t * P:t * P + rows(t)],
                     two[:, (t % 2) * C:(t % 2 + 1) * C].rearrange("p (b n) -> p b n", b=CB)[:, :, 0:rows(t)])\
                    .then_inc(yb_hi, 1)
            act.wait_ge(mix_ps, TILES)
            for t in range(TILES):
                p = a["p_prompt"][0, 0, t * P:(t + 1) * P] if t < TILES - 1 else a["p_sample"][0].rearrange("b s d -> (b s) d")
                act.dma_start(PN[0:rows(t), t, :], p).then_inc(p_in, 16)
            act.wait_ge(var_done, 2)
            nc.scalar.activation(lr[:, 1, 0:TILES], lr[:, 1, 0:TILES], ACT.Sqrt).then_inc(sd_done, 1)
            for t in range(TILES):
                r = rows(t)
                ya = wide[:, (t % 2) * C:(t % 2 + 1) * C].rearrange("p (b n) -> p b n", b=CB)
                act.wait_ge(cc_ps, t + 1)
                if t >= 2:
                    act.wait_ge(ya_lo, t - 1)
                for b in range(CB):
                    nc.scalar.activation(ya[:, b, 0:r], bank[(7, 1)[t % 2]][:, b * P:b * P + r], ACT.Silu,
                                         scale=vecs[:, b, WIDTH + 1:WIDTH + 2], bias=vecs[:, b, WIDTH + 2:WIDTH + 3])\
                        .then_inc(ya_silu, 1)
                act.wait_ge(ya_silu, CB * (t + 1))
                copy(ahi[:, 0:CB, t * P:t * P + r], ya[:, :, 0:r]).then_inc(ya_hi, 1)
            act.wait_ge(state_ps, 1)
            copy(work[0:HIST, 0:C], bank[6][0:HIST, :]).then_inc(state_sb, 1)
            act.wait_ge(state_ps, 2)
            copy(work[0:SAMPLE, C:2 * C], bank[0][0:SAMPLE, :]).then_inc(state_sb, 1)
            load_gain("norm_ffn_g")
            for n in range(11, 15):
                split_high(n)
            for t in range(TILES):
                act.wait_ge(pt_ps, t + 1)
                copy(phi[:, :, t * P:t * P + rows(t)],
                     bank[(1, 7)[t % 2]][:, 0:2 * P].rearrange("p (c n) -> p c n", c=2)[:, :, 0:rows(t)]).then_inc(pt_hi, 1)
            act.wait_ge(store, 16 * (3 + DEC_BATCH))
            for t in range(TILES):
                act.wait_ge(o_add, 3 * TILES + t + 1)
                act.wait_ge(sq_done, TILES + t)
                square(t, FFN)
            root(FFN)
            for t in range(TILES):
                act.wait_ge(norm_done, TILES + t + 1)
                act.dma_start(normed[t * P:t * P + rows(t), :], two[0:rows(t), (t % 2) * D:(t % 2 + 1) * D])\
                   .then_inc(normed_out[t % 2], 16)
                act.wait_ge(rt_ps, t + 1)
                if t > 0:
                    act.wait_ge(r_ps, t)
                copy(wide[:, :].rearrange("p (c n) -> p c n", c=DC)[:, :, 0:rows(t)],
                     pair[(0, 3)[t % 2]][:, :].rearrange("p (c n) -> p c n", c=DC)[:, :, 0:rows(t)]).then_inc(rt_sb, 1)
            load_gain("norm_ple_g")
            for i in range(2):
                act.wait_ge(arg_done, i + 1)
                arg = r4[:, 0, :, :] if i == 0 else r1[:, 2, :]
                nc.scalar.activation(arg, arg, ACT.Exp).then_inc(exp_done, 1)
            for t in range(TILES):
                act.wait_ge(pp_ps, t + 1)
                copy(PP[0:rows(t), t, :], pair[(0, 3)[t % 2]][0:rows(t), :]).then_inc(pp_sb, 1)

            def gather_high(e0, d=0):
                act.wait_ge(g_ps, e0 + 1 + d)
                copy(xhi, pair[1][:, :].rearrange("p (c n) -> p c n", c=DC)).then_inc(g_hi, 1)

            def silu_of(e0, d=0):
                wait_used(act, N_MOE + 1 if e0 == 0 else step_unit(e0, 1), d)
                if e0 > 0:
                    act.wait_ge(hid_done, e0 + d)
                nc.scalar.activation(silu, bank[0], ACT.Silu).then_inc(silu_done, 1)

            def hidden_high(e0, d=0):
                act.wait_ge(t_ps, e0 + 1 + d)
                copy(thi, bank[4].rearrange("p (c n) -> p c n", c=CB)).then_inc(t_hi, 1)

            def result(n, e0, d=0):
                wait_used(act, n, d)
                if e0 > 0:
                    act.wait_ge(scattered, 16 * (e0 + d))
                copy(res[:, 0:C], bank[6]).then_inc(res_act, 1)

            def step(e0, d=0):
                if e0 == 0:
                    split_high(N_MOE + 2)
                    split_high(N_MOE + 3)
                    silu_of(0)
                    split_high(N_STEP)
                    gather_high(1)
                    split_high(N_STEP + 1)
                    hidden_high(0)
                    return
                for k in range(2, 5):
                    split_high(step_unit(e0, k), d)
                silu_of(e0, d)
                split_high(step_unit(e0, 5), d)
                if e0 < EXPERTS - 1:
                    gather_high(e0 + 1, d)
                split_high(step_unit(e0, 6), d)
                split_high(step_unit(e0, 7), d)
                hidden_high(e0, d)
                result(step_unit(e0, 5), e0 - 1, d)

            gather_high(0)
            step(0)
            step(1)
            with act.Fori(0, EXPERTS - 3) as d:
                step(2, d)
            step(EXPERTS - 1)
            result(N_GATE - 1, EXPERTS - 1)

            act.wait_ge(jobs_done, 1)
            jobs_n = act.value_load(jobs_i[0:1, 2 * OVERFLOW_MAX:], min_val=0, max_val=OVERFLOW_MAX)
            with act.If(jobs_n > 0):
                with act.Fori(0, jobs_n) as j:
                    act.wait_ge(v_gps, j + 1)
                    copy(wide[:, :], pair[1][:, :]).then_inc(v_gsb, 1)
                    act.wait_ge(v_gu, j + 1)
                    nc.scalar.activation(silu, bank[0], ACT.Silu).then_inc(v_silu, 1)
                    act.wait_ge(v_tps, j + 1)
                    copy(wide[:, 0:C], bank[4]).then_inc(v_tsb, 1)
                    act.wait_ge(v_dps, j + 1)
                    copy(res, pair[3][:, :]).then_inc(v_res, 1)
            for n in range(N_GATE, N_GATE + SPLIT):
                split_high(n)
            for t in range(TILES):
                act.wait_ge(pair_add, 2 * t + 2)
                act.wait_ge(sq_done, 2 * TILES + t)
                square(t, GATE)
            root(GATE)
            for t in range(TILES):
                normed_high(t, GATE)
            act.wait_ge(norm_done, 3 * TILES)
            load_gain("norm_final_g")
            for q in range(TILES * D // UC):
                i, t = divmod(q, TILES)
                act.wait_ge(s_ps, q + 1)
                if q >= 4:
                    act.wait_ge(s_add, q - 3)
                nc.scalar.activation(wide[0:rows(t), (q % 4) * UC:(q % 4 + 1) * UC], bank[4 + q % 4][0:rows(t), 0:UC],
                                     ACT.Sigmoid).then_inc(s_sig, 1)
                if q == TILES - 1:
                    split_high(N_GATE + SPLIT)
            for t in range(TILES):
                act.wait_ge(s_add, 3 * TILES + t + 1)
                act.wait_ge(sq_done, 3 * TILES + t)
                square(t, FINAL)
            root(FINAL)

        @block.vector
        def _(v):
            own = [0]

            def link(ins):
                ins.then_inc(dve, 1)
                own[0] += 1
                v.wait_ge(dve, own[0])

            def inverse_root(w):
                v.wait_ge(sq_done, TILES * (w + 1))
                nc.vector.tensor_scalar(rs[:, w, 0:TILES], sq[:, w, 0:TILES], 1.0 / D, EPS, ALU.mult, ALU.add)\
                    .then_inc(mean_done, 1)
                v.wait_ge(root_done, w + 1)
                link(nc.vector.reciprocal(rs[:, w, 0:TILES], rs[:, w, 0:TILES]))

            def apply_norm(t, w, to):
                r = rows(t)
                return nc.vector.scalar_tensor_tensor(out=to[0:r], in0=H[0:r, t, :], scalar=rs[0:r, w, t:t + 1],
                                                      in1=gain[0:r, :], op0=ALU.mult, op1=ALU.mult)

            def normed_low(t, w):
                r = rows(t)
                v.wait_ge(xt_hi, (0 if w == MIX else TILES) + t + 1)
                nc.vector.tensor_tensor(alo[:, :, t * P:t * P + r],
                                        pair[t % 2][:, :].rearrange("p (c n) -> p c n", c=DC)[:, :, 0:r],
                                        ahi[:, :, t * P:t * P + r].bitcast(F32), ALU.subtract).then_inc(xt_lo, 1)

            inverse_root(MIX)
            v.wait_ge(gain_in, 16)
            for t in range(TILES):
                apply_norm(t, MIX, H[:, t, :]).then_inc(norm_done, 1)
            for t in range(TILES):
                normed_low(t, MIX)

            def glu(b):
                v.wait_ge(sig_done, b + 1)
                val = pair[2 * (b % 2)][:, :].rearrange("p (s n) -> p s n", s=2)
                cut = SEQ - HALF
                nc.vector.tensor_tensor(G[:, b, HIST:HIST + HALF], val[:, 0, 0:HALF], sg[:, 0:HALF],
                                        ALU.mult).then_inc(glu_done, 1)
                nc.vector.tensor_tensor(G[:, b, HIST + HALF:GP], val[:, 1, 0:cut], sg[:, HALF:SEQ],
                                        ALU.mult).then_inc(glu_done, 1)
                nc.vector.tensor_tensor(GSAM[:, b, :, HIST:], val[:, 1, cut:HALF].rearrange("p (s k) -> p s k", k=DEC_SEQ),
                                        sg[:, SEQ:].rearrange("p (s k) -> p s k", k=DEC_SEQ), ALU.mult)\
                    .then_inc(glu_done, 1)

            def first_tap(b):
                v.wait_ge(glu_done, 3 * b + 3)
                w, bias = vecs[:, b, 0:1], vecs[:, b, WIDTH:WIDTH + 1]
                nc.vector.tensor_scalar(A[:, b, 0:SEQ], G[:, b, 0:SEQ], w, bias, ALU.mult, ALU.add).then_inc(acc_p, 1)
                nc.vector.tensor_scalar(A[:, b, SEQ:].rearrange("p (s k) -> p s k", k=DEC_SEQ), GSAM[:, b, :, 0:DEC_SEQ],
                                        w, bias, ALU.mult, ALU.add).then_inc(acc_s, 1)

            def taps(b, first, last):
                with v.Fori(first, last) as k:
                    w = vecs[:, b, bass.ds(k, 1)]
                    v.wait_ge(acc_p, WIDTH * b + k)
                    nc.vector.scalar_tensor_tensor(out=A[:, b, 0:SEQ], in0=G[:, b, bass.ds(k, SEQ)], scalar=w,
                                                   in1=A[:, b, 0:SEQ], op0=ALU.mult, op1=ALU.add).then_inc(acc_p, 1)
                    v.wait_ge(acc_s, WIDTH * b + k)
                    sam = A[:, b, SEQ:].rearrange("p (s k) -> p s k", k=DEC_SEQ)
                    nc.vector.scalar_tensor_tensor(out=sam, in0=GSAM[:, b, :, bass.ds(k, DEC_SEQ)], scalar=w,
                                                   in1=sam, op0=ALU.mult, op1=ALU.add).then_inc(acc_s, 1)

            def variance(which):
                link(nc.vector.tensor_scalar(lr[:, which, 0:TILES], mv[:, which, :, 1], EPS, None, ALU.add))
                nc.vector.tensor_scalar(lr[:, which, 0:TILES], lr[:, which, 0:TILES], 0.0, None, ALU.max)\
                    .then_inc(var_done, 1)
                v.wait_ge(sd_done, which + 1)
                link(nc.vector.reciprocal(lr[:, which, 0:TILES], lr[:, which, 0:TILES]))

            v.wait_ge(const, N_CONST)
            v.wait_ge(setup_sb, 1 + 2 * CB)
            MID = WIDTH // 2 + 1
            glu(0)
            first_tap(0)
            taps(0, 1, MID)
            glu(1)
            taps(0, MID, WIDTH)
            glu(2)
            first_tap(1)
            taps(1, 1, MID)
            glu(3)
            taps(1, MID, WIDTH)
            first_tap(2)
            taps(2, 1, WIDTH)
            v.wait_ge(v_gelu, 2 * TILES)
            for t in range(TILES):
                r = rows(t)
                link(nc.vector.bn_stats(st[0:r, 0, t, 0:6], V[0:r, t, :]))
                link(nc.vector.bn_aggr(mv[0:r, 0, t, :], st[0:r, 0, t, 0:6]))
            variance(0)
            for t in range(TILES):
                r = rows(t)
                nc.vector.tensor_scalar(V[0:r, t, :], V[0:r, t, :], mv[0:r, 0, t, 0:1], lr[0:r, 0, t:t + 1],
                                        ALU.subtract, ALU.mult).then_inc(v_norm, 1)
            v.wait_ge(slots_clear, 16)
            first_tap(3)
            taps(3, 1, WIDTH)
            v.wait_ge(u_gelu, CB)
            for t in range(TILES):
                r = rows(t)
                v.wait_ge(mix_ps, t + 1)
                if t >= 2:
                    v.wait_ge(yb_lo, t - 1)
                    v.wait_ge(yb_hi, t - 1)
                yb = two[:, (t % 2) * C:(t % 2 + 1) * C].rearrange("p (b n) -> p b n", b=CB)[:, :, 0:r]
                nc.vector.tensor_tensor(yb, bank[t % 2].rearrange("p (b n) -> p b n", b=CB)[:, :, 0:r],
                                        U[:, :, t * P:t * P + r], ALU.mult).then_inc(yb_mul, 1)
                v.wait_ge(yb_hi, t + 1)
                nc.vector.tensor_tensor(alo[:, CB:, t * P:t * P + r], yb, ahi[:, CB:, t * P:t * P + r].bitcast(F32),
                                        ALU.subtract).then_inc(yb_lo, 1)
            for t in range(TILES):
                r = rows(t)
                v.wait_ge(ct_ps, t + 1)
                link(nc.vector.bn_stats(st[0:r, 1, t, 0:6], bank[2 + t][0:r, :]))
                link(nc.vector.bn_aggr(mv[0:r, 1, t, :], st[0:r, 1, t, 0:6]))
            variance(1)
            for t in range(TILES):
                r = rows(t)
                if t >= 2:
                    v.wait_ge(cc_ps, t - 1)
                nc.vector.tensor_scalar(two[0:r, D + (t % 2) * C:D + (t % 2 + 1) * C], bank[2 + t][0:r, :],
                                        mv[0:r, 1, t, 0:1], lr[0:r, 1, t:t + 1], ALU.subtract, ALU.mult)\
                    .then_inc(ct_norm, 1)
            for t in range(TILES):
                r = rows(t)
                v.wait_ge(ya_hi, t + 1)
                nc.vector.tensor_tensor(alo[:, 0:CB, t * P:t * P + r],
                                        wide[:, (t % 2) * C:(t % 2 + 1) * C].rearrange("p (b n) -> p b n", b=CB)[:, :, 0:r],
                                        ahi[:, 0:CB, t * P:t * P + r].bitcast(F32), ALU.subtract).then_inc(ya_lo, 1)
            v.wait_ge(x_again, 16 * TILES)
            for q in range(TILES * D // UC):
                i, t = divmod(q, TILES)
                at = H[0:rows(t), t, i * UC:(i + 1) * UC]
                v.wait_ge(o_ps, q + 1)
                nc.vector.tensor_tensor(at, bank[2 + q % 4][0:rows(t), 0:UC], at, ALU.add).then_inc(o_add, 1)
            for t in range(TILES):
                v.wait_ge(pt_hi, t + 1)
                nc.vector.tensor_tensor(plo[:, :, t * P:t * P + rows(t)],
                                        bank[(1, 7)[t % 2]][:, 0:2 * P].rearrange("p (c n) -> p c n", c=2)[:, :, 0:rows(t)],
                                        phi[:, :, t * P:t * P + rows(t)].bitcast(F32), ALU.subtract).then_inc(pt_lo, 1)
            inverse_root(FFN)
            v.wait_ge(gain_in, 32)
            for t in range(TILES):
                if t >= 2:
                    v.wait_ge(normed_out[t % 2], 16 * (t // 2))
                    v.wait_ge(rt_ps, t - 1)
                apply_norm(t, FFN, two[:, (t % 2) * D:(t % 2 + 1) * D]).then_inc(norm_done, 1)

            v.wait_ge(small_in, 16 * 5)
            v.wait_ge(r_ps, TILES)
            NL = GROUPS + EXPERTS
            logits = bank[2][:, 0:TILES * NL].rearrange("p (t n) -> p t n", t=TILES)
            full = TILES - 1
            link(nc.vector.tensor_tensor(lg[:, 0:full, :], logits[:, 0:full, :],
                                         rb[:, :].unsqueeze(1).to_broadcast([P, full, NL]), ALU.add))
            link(nc.vector.tensor_tensor(lg[0:SAMPLE, full, :], logits[0:SAMPLE, full, :], rb[0:SAMPLE, :], ALU.add))
            v.sem_inc(lg_sb, 1)
            gl = lg[:, :, 0:GROUPS]
            el = lg[:, :, GROUPS:].rearrange("p t (g k) -> p t g k", g=GROUPS)

            def over(x, n=GROUPS):
                return x.unsqueeze(2).to_broadcast([P, TILES, n])

            def first_max(values, top, hot, tmp):
                link(nc.vector.tensor_reduce(top, values, AX_X, ALU.max))
                link(nc.vector.tensor_tensor(tmp, values, over(top), ALU.is_equal))
                link(nc.vector.tensor_tensor(tmp, tmp, rev[:, :].unsqueeze(1).to_broadcast([P, TILES, GROUPS]), ALU.mult))
                link(nc.vector.tensor_reduce(r1[:, 15, :], tmp, AX_X, ALU.max))
                link(nc.vector.tensor_tensor(hot, tmp, over(r1[:, 15, :]), ALU.is_equal))

            gmax, gsum, diff, gw, m1, m2, den, w1, w2 = (r1[:, i, :] for i in range(9))
            diff = r1[:, 2, :]
            egl, hot_g, elg, hot1, hot2, tmp4, rest = (r4[:, i, :, :] for i in range(7))
            M1, M2, M, earlier, spare, spare2 = (r16[:, i, :, :] for i in range(6))

            def by_group(x):
                return x.rearrange("p t (g k) -> p t g k", g=GROUPS)

            first_max(gl, gmax, hot_g, tmp4)
            nc.vector.tensor_tensor(egl, gl, over(gmax), ALU.subtract).then_inc(arg_done, 1)
            hot_gk = hot_g.unsqueeze(3).to_broadcast([P, TILES, GROUPS, PER])
            link(nc.vector.tensor_tensor(by_group(spare), el, hot_gk, ALU.mult))
            link(nc.vector.tensor_reduce(elg, spare.rearrange("p t (g k) -> p t k g", g=GROUPS), AX_X, ALU.add))
            first_max(elg, m1, hot1, tmp4)
            link(nc.vector.scalar_tensor_tensor(out=rest, in0=hot1, scalar=-BIG, in1=elg, op0=ALU.mult, op1=ALU.add))
            first_max(rest, m2, hot2, tmp4)
            nc.vector.tensor_tensor(diff, m2, m1, ALU.subtract).then_inc(arg_done, 1)
            for hot, m in ((hot1, M1), (hot2, M2)):
                link(nc.vector.tensor_tensor(by_group(m), hot_gk,
                                             hot.unsqueeze(2).to_broadcast([P, TILES, GROUPS, PER]), ALU.mult))
            link(nc.vector.tensor_tensor(M, M1, M2, ALU.add))
            link(nc.vector.memset(M[SAMPLE:, full, :], 0.0))
            link(nc.vector.memset(earlier[:, 0, :], 0.0))
            for t in range(1, TILES):
                link(nc.vector.tensor_tensor(earlier[:, t, :], earlier[:, t - 1, :], M[:, t - 1, :], ALU.add))
            nc.vector.tensor_tensor(spare2[:, 0, :], earlier[:, full, :], M[:, full, :], ALU.add).then_inc(onehot, 1)
            v.wait_ge(exp_done, 2)
            link(nc.vector.tensor_reduce(gsum, egl, AX_X, ALU.add))
            link(nc.vector.reciprocal(gw, gsum))
            link(nc.vector.tensor_scalar(den, diff, 1.0, None, ALU.add))
            link(nc.vector.reciprocal(den, den))
            link(nc.vector.tensor_tensor(w1, den, gw, ALU.mult))
            link(nc.vector.tensor_tensor(w2, w1, diff, ALU.mult))
            v.wait_ge(rank_ps, 1)
            link(nc.vector.tensor_tensor(spare, bank[5][:, 0:TILES * EXPERTS].rearrange("p (t e) -> p t e", t=TILES),
                                         base[:, :].unsqueeze(1).to_broadcast([P, TILES, EXPERTS]), ALU.add))
            for k, m in enumerate((M1, M2)):
                link(nc.vector.tensor_tensor(m, m, spare, ALU.mult))
                link(nc.vector.tensor_reduce(r1[:, 9 + k, :], m, AX_X, ALU.add))
                nc.vector.tensor_copy(pos[:, :, k], r1[:, 9 + k, :]).then_inc(dve, 1)
                own[0] += 1
            v.wait_ge(dve, own[0])
            v.sem_inc(slot_at, 1)
            counts = bank[5][0:1, P:P + EXPERTS]
            for t in range(4):
                link(nc.vector.tensor_scalar(wl[:, 0, t * EXPERTS:(t + 1) * EXPERTS], counts, float(P * (t + 1)), None,
                                             ALU.is_gt))
            link(nc.vector.tensor_tensor_scan(wl[:, 1, :], wl[:, 0, :], wl[:, 2, :], 0.0, ALU.add, ALU.add))
            for j in range(OVERFLOW_MAX):
                link(nc.vector.scalar_tensor_tensor(out=wl8[:, 0, j, :], in0=wl[:, 1, :], scalar=float(j + 1),
                                                    in1=wl[:, 0, :], op0=ALU.is_equal, op1=ALU.mult))
            for q in range(2):
                link(nc.vector.tensor_tensor(wl8[:, 1, :, :], wl8[:, 0, :, :],
                                             codes[:, q, :].unsqueeze(1).to_broadcast([1, OVERFLOW_MAX, 4 * EXPERTS]),
                                             ALU.mult))
                link(nc.vector.tensor_reduce(jobs[:, q * OVERFLOW_MAX:(q + 1) * OVERFLOW_MAX], wl8[:, 1, :, :], AX_X, ALU.add))
            link(nc.vector.tensor_copy(jobs[:, 2 * OVERFLOW_MAX:], wl[:, 1, 4 * EXPERTS - 1:]))
            nc.vector.tensor_copy(jobs_i[:, :], jobs[:, :]).then_inc(jobs_done, 1)

            def split_low(n, d=0):
                v.wait_ge(hi_done, n + 1 + 6 * d)
                wait_used(v, n - SPLIT, d)
                s = slice(0, UNIT - LOW_POOL)
                nc.vector.tensor_tensor(lo[:, n % SPLIT, s], raw[:, n % RAW, s], hi[:, n % SPLIT, s].bitcast(F32),
                                        ALU.subtract).then_inc(lo_dve, 1)

            def hidden(e0, d=0):
                v.wait_ge(silu_done, e0 + 1 + d)
                wait_used(v, N_MOE + 3 if e0 == 0 else step_unit(e0, 3), d)
                if e0 > 0:
                    v.wait_ge(t_ps, e0 + d)
                nc.vector.tensor_tensor(hid, bank[1], silu, ALU.mult).then_inc(hid_done, 1)

            def gather_low(e0, d=0):
                v.wait_ge(g_hi, e0 + 1 + d)
                nc.vector.tensor_tensor(xlo, pair[1][:, :].rearrange("p (c n) -> p c n", c=DC), xhi.bitcast(F32),
                                        ALU.subtract).then_inc(g_lo, 1)

            def hidden_low(e0, d=0):
                v.wait_ge(t_hi, e0 + 1 + d)
                nc.vector.tensor_tensor(tlo, bank[4].rearrange("p (c n) -> p c n", c=CB), thi.bitcast(F32),
                                        ALU.subtract).then_inc(t_lo, 1)

            def result(n, e0, d=0):
                wait_used(v, n, d)
                if e0 > 0:
                    v.wait_ge(scattered, 16 * (e0 + d))
                nc.vector.tensor_copy(res[:, C:], bank[7]).then_inc(res_dve, 1)

            def step(e0, d=0):
                if e0 == 0:
                    split_low(N_MOE + 2)
                    split_low(N_MOE + 3)
                    hidden(0)
                    gather_low(1)
                    split_low(N_STEP)
                    split_low(N_STEP + 1)
                    hidden_low(0)
                    return
                for k in range(2, 6):
                    split_low(step_unit(e0, k), d)
                hidden(e0, d)
                if e0 < EXPERTS - 1:
                    gather_low(e0 + 1, d)
                split_low(step_unit(e0, 6), d)
                split_low(step_unit(e0, 7), d)
                hidden_low(e0, d)
                result(step_unit(e0, 5), e0 - 1, d)

            split_low(N_MOE)
            split_low(N_MOE + 1)
            gather_low(0)
            step(0)
            step(1)
            with v.Fori(0, EXPERTS - 3) as d:
                step(2, d)
            step(EXPERTS - 1)
            result(N_GATE - 1, EXPERTS - 1)

            v.wait_ge(jobs_done, 1)
            jobs_n = v.value_load(jobs_i[0:1, 2 * OVERFLOW_MAX:], min_val=0, max_val=OVERFLOW_MAX)
            with v.If(jobs_n > 0):
                with v.Fori(0, jobs_n) as j:
                    v.wait_ge(v_silu, j + 1)
                    nc.vector.tensor_tensor(hid, bank[1], silu, ALU.mult).then_inc(v_hid, 1)

            for t in range(TILES):
                r = rows(t)
                v.wait_ge(pair_in, 16 * (t + 1))
                for k, w in enumerate((w1, w2)):
                    if k:
                        v.wait_ge(pair_add, 2 * t + 1)
                    nc.vector.scalar_tensor_tensor(out=H[0:r, t, :], in0=two[0:r, k * D:(k + 1) * D],
                                                   scalar=w[0:r, t:t + 1], in1=H[0:r, t, :], op0=ALU.mult,
                                                   op1=ALU.add).then_inc(pair_add, 1)
            inverse_root(GATE)
            v.wait_ge(gain_in, 48)
            for t in range(TILES):
                if t >= 2:
                    v.wait_ge(xt_ps, TILES + t - 1)
                apply_norm(t, GATE, two[:, (t % 2) * D:(t % 2 + 1) * D]).then_inc(norm_done, 1)
                if t >= 1:
                    normed_low(t - 1, GATE)
            normed_low(TILES - 1, GATE)
            for q in range(TILES * D // UC):
                i, t = divmod(q, TILES)
                r = rows(t)
                s = wide[0:r, (q % 4) * UC:(q % 4 + 1) * UC]
                at = H[0:r, t, i * UC:(i + 1) * UC]
                v.wait_ge(s_sig, q + 1)
                nc.vector.tensor_tensor(s, s, PP[0:r, t, i * UC:(i + 1) * UC], ALU.mult).then_inc(s_mul, 1)
                v.wait_ge(s_mul, q + 1)
                nc.vector.tensor_tensor(at, at, s, ALU.add).then_inc(s_add, 1)
            inverse_root(FINAL)
            v.wait_ge(gain_in, 64)
            for t in range(TILES):
                if t >= 2:
                    v.wait_ge(y_out[t % 2], 16 * (t // 2))
                apply_norm(t, FINAL, two[:, (t % 2) * D:(t % 2 + 1) * D]).then_inc(y_sb, 1)

        @block.tensor
        def _(pe):
            mm, tr = nc.tensor.matmul, nc.tensor.transpose

            def wait_unit(n, d=0):
                pe.wait_ge(hi_done, n + 1 + 6 * d)
                pe.wait_ge(lo_pool, n + 1 + 6 * d)
                if N_MOE <= n < N_GATE:
                    pe.wait_ge(lo_dve, n - N_MOE + 1 + 6 * d)

            def split_product(out_, x_hi, x_lo, w_hi, w_lo, start, stop):
                mm(out_, x_hi, w_hi, start=start, stop=False)
                mm(out_, x_hi, w_lo, start=False, stop=False)
                return mm(out_, x_lo, w_hi, start=False, stop=stop)

            def unit(n, c):
                return (s[:, n % SPLIT, :].rearrange("p (c n) -> p c n", c=c) for s in (hi, lo))

            def transpose_rows(src, r, to):
                for c in range(DC):
                    ins = tr(to[:, c * P:c * P + r], src[0:r, c * P:(c + 1) * P], ident[0:r, 0:r])
                return ins

            def normed_tiles(w, src):
                for t in range(TILES):
                    first = 0 if w == MIX else TILES
                    pe.wait_ge(norm_done, w * TILES + t + 1)
                    if t >= 2:
                        pe.wait_ge(xt_lo, first + t - 1)
                    transpose_rows(src(t), rows(t), pair[t % 2]).then_inc(xt_ps, 1)

            pe.wait_ge(const, 2)
            pe.wait_ge(rows_in, 16 * 6)
            for b in range(CB):
                ins = tr(bank[4][:, b * P:b * P + NV], vrow[0:NV, b * P:(b + 1) * P], ident[0:NV, 0:NV])
            ins.then_inc(setup_ps, 1)
            for i in range(2):
                for b in range(CB):
                    ins = tr(bank[5 + i][:, b * P:b * P + SROWS], stn[0:SROWS, i, b * P:(b + 1) * P],
                             ident[0:SROWS, 0:SROWS])
                ins.then_inc(setup_ps, 1)
            normed_tiles(MIX, lambda t: H[:, t, :])

            def channel_block(n, half, banks, bank_sem):
                w_hi, w_lo = unit(n, DC)
                cols = slice(half * P, (half + 1) * P)
                outs = [banks[:, s * 512:s * 512 + HALF] for s in range(2)]
                for c in range(DC):
                    for w, x, last in ((w_hi, ahi, False), (w_hi, alo, False), (w_lo, ahi, True)):
                        for s in range(2):
                            ins = mm(outs[s], w[:, c, cols], x[:, c, s * HALF:(s + 1) * HALF],
                                     start=(c == 0 and w is w_hi and x is ahi), stop=(c == DC - 1 and last))
                ins.then_inc(bank_sem, 1)

            pe.wait_ge(xt_lo, TILES)
            pe.wait_ge(setup_sb, 1 + 2 * CB)
            for b in range(CB):
                n = 2 * (b // 2)
                if b % 2 == 0:
                    wait_unit(n)
                if b >= 2:
                    pe.wait_ge(glu_done, 3 * (b - 1))
                channel_block(n, b % 2, pair[2 * (b % 2)], z_ps)
                if b % 2 == 0:
                    wait_unit(n + 1)
                channel_block(n + 1, b % 2, pair[2 * (b % 2) + 1], z_ps)

            def token_rows(q, n, to, i_sem, x_hi=ahi, x_lo=alo):
                t = q % TILES
                r = rows(t)
                w_hi, w_lo = unit(n, DC)
                for c in range(DC):
                    ins = split_product(to[0:r, 0:UC], x_hi[:, c, t * P:t * P + r], x_lo[:, c, t * P:t * P + r],
                                        w_hi[:, c, :], w_lo[:, c, :], c == 0, c == DC - 1)
                return ins.then_inc(i_sem, 1)

            pe.wait_ge(glu_done, 9)
            for q in range(2 * TILES):
                n = 4 + q // TILES
                if q % TILES == 0:
                    wait_unit(n)
                if q >= 4:
                    pe.wait_ge(v_gelu, q - 3)
                token_rows(q, n, bank[q % 4], v_ps)
            pe.wait_ge(glu_done, 12)
            for b in range(CB):
                n = 6 + b // 2
                if b % 2 == 0:
                    wait_unit(n)
                if b >= 2:
                    pe.wait_ge(u_gelu, b - 1)
                channel_block(n, b % 2, pair[2 + b % 2], u_ps)
            pe.wait_ge(masked, 2)
            pe.wait_ge(v_gelu, 2 * TILES)
            for i in range(HEADS):
                ins = tr(pair[0][:, i * P:(i + 1) * P], wsn[:, i, :], ident[:, :])
            ins.then_inc(setup_ps, 1)
            for i in range(HEADS):
                ins = tr(bank[2][0:SAMPLE, i * SAMPLE:(i + 1) * SAMPLE], wssn[0:SAMPLE, i, :], ident[0:SAMPLE, 0:SAMPLE])
            ins.then_inc(setup_ps, 1)
            pe.wait_ge(setup_sb, 3 + 2 * CB)
            pe.wait_ge(small_in, 16 * 5)
            for t in range(TILES):
                r = rows(t)
                pe.wait_ge(v_ready, t + 1)
                if t >= 2:
                    pe.wait_ge(yb_mul, t - 1)
                for i in range(HEADS):
                    at = (i % 2) * HD
                    to = bank[t % 2][at:at + HD, (i // 2) * P:(i // 2) * P + r]
                    w = WS[0:r, i, 0:r] if t < TILES - 1 else WSS[0:r, i, :]
                    mm(to, V[0:r, t, i * HD:(i + 1) * HD], w, start=True, stop=False)
                    if t < TILES - 1:
                        ins = mm(to, ones[BS:BS + 1, 0:HD], bs[:, i * P:(i + 1) * P], start=False, stop=True)
                    else:
                        b_row = bs[:, i * P:i * P + DEC_SEQ].unsqueeze(1).to_broadcast([1, DEC_BATCH, DEC_SEQ])
                        ins = mm(to, ones[BS:BS + 1, 0:HD], b_row, start=False, stop=True)
                ins.then_inc(mix_ps, 1)
            pe.wait_ge(acc_p, WIDTH * CB)
            pe.wait_ge(acc_s, WIDTH * CB)
            pe.wait_ge(u_gelu, CB)
            for t in range(TILES):
                for b in range(CB):
                    ins = tr(bank[2 + t][0:rows(t), b * P:(b + 1) * P], A[:, b, t * P:t * P + rows(t)], ident[:, :])
                ins.then_inc(ct_ps, 1)
            pe.wait_ge(yb_mul, TILES)
            for t in range(TILES):
                r = rows(t)
                pe.wait_ge(ct_norm, t + 1)
                if t >= 2:
                    pe.wait_ge(ya_silu, CB * (t - 1))
                for b in range(CB):
                    at = D + (t % 2) * C + b * P
                    ins = tr(bank[(7, 1)[t % 2]][:, b * P:b * P + r], two[0:r, at:at + P], ident[0:r, 0:r])
                ins.then_inc(cc_ps, 1)
            pe.wait_ge(fresh_done, 1)
            for b in range(CB):
                ins = tr(bank[6][0:HIST, b * P:(b + 1) * P], G[:, b, GP - HIST:GP], ident[:, :])
            ins.then_inc(state_ps, 1)
            for b in range(CB):
                ins = tr(bank[0][0:SAMPLE, b * P:(b + 1) * P], fresh[:, b, :], ident[:, :])
            ins.then_inc(state_ps, 1)
            pe.wait_ge(yb_lo, TILES)
            for q in range(TILES * D // UC):
                n = N_OUT + q // TILES
                if q % TILES == 0:
                    wait_unit(n)
                if q < TILES:
                    pe.wait_ge(ya_lo, q + 1)
                if q >= 4:
                    pe.wait_ge(o_add, q - 3)
                token_rows(q, n, bank[2 + q % 4], o_ps)
            pe.wait_ge(p_in, 16 * TILES)
            for t in range(TILES):
                r = rows(t)
                if t >= 2:
                    pe.wait_ge(pt_lo, t - 1)
                for c in range(2):
                    ins = tr(bank[(1, 7)[t % 2]][:, c * P:c * P + r], PN[0:r, t, c * P:(c + 1) * P], ident[0:r, 0:r])
                ins.then_inc(pt_ps, 1)
            pe.wait_ge(pt_lo, TILES)
            pe.wait_ge(state_sb, 2)
            pe.wait_ge(o_add, TILES * D // UC)
            NL = GROUPS + EXPERTS
            for t in range(TILES):
                r = rows(t)
                pe.wait_ge(norm_done, TILES + t + 1)
                if t >= 2:
                    pe.wait_ge(rt_sb, t - 1)
                transpose_rows(two[:, (t % 2) * D:(t % 2 + 1) * D], r, pair[(0, 3)[t % 2]]).then_inc(rt_ps, 1)
                pe.wait_ge(rt_sb, t + 1)
                for c in range(DC):
                    ins = mm(bank[2][0:r, t * NL:(t + 1) * NL], wide[:, c * P:c * P + r], wr[:, c, :],
                             start=(c == 0), stop=(c == DC - 1))
                ins.then_inc(r_ps, 1)

            def embedding(t):
                r = rows(t)
                w_hi, w_lo = unit(N_PROJ, 2)
                if t >= 2:
                    pe.wait_ge(pp_sb, t - 1)
                for half in range(2):
                    for c in range(2):
                        s = slice(half * C, (half + 1) * C)
                        ins = split_product(pair[(0, 3)[t % 2]][0:r, s], phi[:, c, t * P:t * P + r],
                                            plo[:, c, t * P:t * P + r], w_hi[:, c, s], w_lo[:, c, s], c == 0, c == 1)
                return ins.then_inc(pp_ps, 1)

            wait_unit(N_PROJ)
            pe.wait_ge(rt_sb, TILES)
            embedding(0)
            embedding(1)
            pe.wait_ge(onehot, 1)
            M, earlier = r16[:, 2, :, :], r16[:, 3, :, :]
            flat = "p t e -> p (t e)"
            mm(bank[5][:, 0:TILES * EXPERTS], before[:, :], M.rearrange(flat), start=True, stop=False)
            mm(bank[5][:, 0:TILES * EXPERTS], ones[:, :], earlier.rearrange(flat), start=False, stop=True)
            mm(bank[5][:, P:P + EXPERTS], ones[:, :], r16[:, 5, 0, :], start=True, stop=True).then_inc(rank_ps, 1)
            for t in range(2, TILES):
                embedding(t)

            def transpose_gathered(e0, d=0):
                pe.wait_ge(gathered, 16 * (e0 + 1) + 16 * d)
                if e0 > 0:
                    pe.wait_ge(g_lo, e0 + d)
                transpose_rows(xg, P, pair[1]).then_inc(g_ps, 1)

            def gate_up(n, e0, d=0):
                pe.wait_ge(g_lo, e0 + 1 + d)
                if e0 > 0:
                    pe.wait_ge(hid_done, e0 + d)
                for k in range(4):
                    wait_unit(n + k, d)
                    w_hi, w_lo = unit(n + k, DC // 2)
                    for c in range(DC // 2):
                        at = (k % 2) * (DC // 2) + c
                        ins = split_product(bank[k // 2], xhi[:, at, :], xlo[:, at, :], w_hi[:, c, :], w_lo[:, c, :],
                                            at == 0, at == DC - 1)
                    ins.then_inc(pe_unit, 1)

            def transpose_hidden(e0, d=0):
                pe.wait_ge(hid_done, e0 + 1 + d)
                if e0 > 0:
                    pe.wait_ge(t_lo, e0 + d)
                for c in range(CB):
                    ins = tr(bank[4][:, c * P:(c + 1) * P], hid[:, c * P:(c + 1) * P], ident[:, :])
                ins.then_inc(t_ps, 1)

            def down(n, e0, d=0):
                pe.wait_ge(t_lo, e0 + 1 + d)
                if e0 > 0:
                    pe.wait_ge(res_act, e0 + d)
                    pe.wait_ge(res_dve, e0 + d)
                for k in range(2):
                    wait_unit(n + k, d)
                    w_hi, w_lo = unit(n + k, 2)
                    for c in range(2):
                        at = 2 * k + c
                        for half in range(2):
                            s = slice(half * C, (half + 1) * C)
                            ins = split_product(bank[6 + half], thi[:, at, :], tlo[:, at, :], w_hi[:, c, s], w_lo[:, c, s],
                                                at == 0, at == CB - 1)
                    ins.then_inc(pe_unit, 1)

            def step(e0, d=0):
                gate_up(N_MOE if e0 == 0 else step_unit(e0, 0), e0, d)
                if e0 < EXPERTS - 1:
                    transpose_gathered(e0 + 1, d)
                if e0 > 0:
                    down(step_unit(e0, 4), e0 - 1, d)
                transpose_hidden(e0, d)

            pe.wait_ge(lg_sb, 1)
            pe.wait_ge(pp_sb, TILES)
            transpose_gathered(0)
            step(0)
            step(1)
            with pe.Fori(0, EXPERTS - 3) as d:
                step(2, d)
            step(EXPERTS - 1)
            down(N_GATE - 2, EXPERTS - 1)

            pe.wait_ge(jobs_done, 1)
            jobs_n = pe.value_load(jobs_i[0:1, 2 * OVERFLOW_MAX:], min_val=0, max_val=OVERFLOW_MAX)
            weights = raw[:, :, :].rearrange("p s n -> p (s n)")
            with pe.If(jobs_n > 0):
                pe.wait_ge(t_lo, EXPERTS)
                pe.wait_ge(res_act, EXPERTS)
                pe.wait_ge(res_dve, EXPERTS)
                with pe.Fori(0, jobs_n) as j:
                    pe.wait_ge(v_in, 16 * j + 16)
                    transpose_rows(xg, P, pair[1]).then_inc(v_gps, 1)
                    pe.wait_ge(v_gsb, j + 1)
                    for i in range(2):
                        pe.wait_ge(v_w[i], 16 * j + 16)
                        for c in range(DC):
                            at = (i * DC + c) * DE
                            ins = mm(bank[i], wide[:, c * P:(c + 1) * P], weights[:, at:at + DE],
                                     start=(c == 0), stop=(c == DC - 1))
                    ins.then_inc(v_gu, 1)
                    pe.wait_ge(v_hid, j + 1)
                    for c in range(CB):
                        ins = tr(bank[4][:, c * P:(c + 1) * P], hid[:, c * P:(c + 1) * P], ident[:, :])
                    ins.then_inc(v_tps, 1)
                    pe.wait_ge(v_tsb, j + 1)
                    pe.wait_ge(v_w[2], 16 * j + 16)
                    for c in range(CB):
                        for half in range(2):
                            at = 2 * DC * DE + c * D + half * C
                            ins = mm(bank[6 + half], wide[:, c * P:(c + 1) * P], weights[:, at:at + C],
                                     start=(c == 0), stop=(c == CB - 1))
                    ins.then_inc(v_dps, 1)

            normed_tiles(GATE, lambda t: two[:, (t % 2) * D:(t % 2 + 1) * D])
            for q in range(TILES * D // UC):
                n = N_GATE + q // TILES
                if q % TILES == 0:
                    wait_unit(n)
                if q < TILES:
                    pe.wait_ge(xt_lo, TILES + q + 1)
                if q >= 4:
                    pe.wait_ge(s_sig, q - 3)
                token_rows(q, n, bank[4 + q % 4], s_ps)


_INS = ["x_prompt", "x_sample", "p_prompt", "p_sample", "state_conv", "norm_mix_g", "w_in", "conv_w", "conv_b",
        "conv_ln_g", "conv_ln_b", "gmlp_ln_g", "gmlp_ln_b", "w_s", "b_s", "w_out", "norm_ffn_g", "w_router_group",
        "b_router_group", "w_router_expert", "b_router_expert", "w_exp_gate", "w_exp_up", "w_exp_down", "norm_ple_g",
        "w_ple_gate", "w_ple_proj", "norm_final_g"]
_OUTS = [("y_prompt", (1, SEQ, D)), ("y_sample", (DEC_BATCH, DEC_SEQ, D)), ("state_conv_prompt", (1, 1, HIST, C)),
         ("state_conv_sample", (1, DEC_BATCH, HIST, C)), ("state_gmlp_v_sample", (1, DEC_BATCH, DEC_SEQ, C))]


def kernel(**inputs):
    import numpy as _np
    import concourse.bacc as _bacc
    from concourse import mybir as _mybir
    from concourse.bass_utils import run_bass_kernel_spmd as _run

    nc = _bacc.Bacc("TRN2", target_bir_lowering=False, num_devices=1)
    arrays, ins, outs = {}, {}, {}
    for name in _INS:
        x = _np.ascontiguousarray(inputs[name])
        arrays[f"in_{name}"] = x
        ins[name] = nc.dram_tensor(f"in_{name}", x.shape, _mybir.dt.from_np(x.dtype), kind="ExternalInput").ap()
    for name, shape in _OUTS:
        outs[name] = nc.dram_tensor(f"out_{name}", shape, _mybir.dt.float32, kind="ExternalOutput").ap()
    hybrid_layer(nc, ins, outs)
    r = _run(nc, [arrays], core_ids=[0])
    return tuple(r.results[0][f"out_{name}"] for name, _ in _OUTS)
```

```python
from contextlib import ExitStack

import concourse.bass as bass
from concourse import mybir

F32 = mybir.dt.float32
F32R = mybir.dt.float32r
U32 = mybir.dt.uint32
ALU = mybir.AluOpType
ACT = mybir.ActivationFunctionType
AX_X = mybir.AxisListType.X

P = 128
D = 1024
SEQ = 512
DEC_BATCH = 8
DEC_SEQ = 8
SAMPLE = DEC_BATCH * DEC_SEQ
TOKENS = SEQ + SAMPLE
TILES = 5
HALF = TOKENS // 2
C = 512
CB = C // P
DC = D // P
HEADS = 8
HD = C // HEADS
WIDTH = 31
HIST = WIDTH - 1
GP = HIST + SEQ
GS = HIST + DEC_SEQ
GROW = GP + DEC_BATCH * GS
PLE = 256
GROUPS = 4
PER = 4
EXPERTS = GROUPS * PER
DE = D // 2
EPS = 1e-6
UNIT = 2048
UC = UNIT // DC
RAW = 6
SPLIT = 3
CAP = TILES * P
NOBODY = 4096
OVERFLOW_MAX = 8
BIG = 3.0e38

Z_COLS = [0, C, UC, C + UC, 3 * C, 3 * C + UC, 2 * C, 2 * C + UC]
N_OUT = len(Z_COLS)
N_PROJ = N_OUT + D // UC
N_MOE = N_PROJ + 1
N_STEP = N_MOE + 4
N_GATE = N_STEP + 6 * (EXPERTS - 1) + 2
N_UNITS = N_GATE + D // UC
PAIR_SLOTS = [(N_UNITS + i) % RAW for i in range(2)]
N_CONST = 16 + 2 * TILES
N_CONST_SQ = 4
LOW_POOL = 512
TAP_BLOCK = 1
DVE_BLOCKS = [b for b in range(CB) if b != TAP_BLOCK]
TAP_CHUNK = 6
TAP_CHUNKS = 2
TAP_PAIRS = (WIDTH - 1 - TAP_CHUNK * TAP_CHUNKS) // 2
FIRST_TAPS = 11
SEQS = 4
WORD_COLS = 2 * EXPERTS * CAP // P
GATE_ORDER = [(i, t) for t in range(TILES) for i in range(SPLIT)] + [(SPLIT, t) for t in range(TILES)]
MIX, FFN, GATE, FINAL = range(4)


def rows(t):
    return P if t < TILES - 1 else SAMPLE


def hybrid_layer(nc, a, out):
    ctx = ExitStack()

    def sb(name, shape, dt=F32):
        return ctx.enter_context(nc.sbuf_tensor(name, shape, dt))

    def sem(name):
        return ctx.enter_context(nc.semaphore(name))

    with ctx:
        raw = sb("raw", [P, RAW, UNIT])
        hi = sb("hi", [P, SPLIT, UNIT], F32R)
        lo = sb("lo", [P, SPLIT, UNIT], F32R)
        act_hi = sb("act_hi", [P, DC * TOKENS], F32R)
        act_lo = sb("act_lo", [P, DC * TOKENS], F32R)
        h = sb("h", [P, TILES * D])
        conv = sb("conv", [P, CB * (GROW + TOKENS)])
        ws = sb("ws", [P, HEADS * (P + SAMPLE)])
        wide = sb("wide", [P, D])
        two = sb("two", [P, 2 * D])
        work = sb("work", [P, D])
        gain = sb("gain", [P, D])
        ident = sb("ident", [P, P])
        before = sb("before", [P, P])
        ones = sb("ones", [P, P])
        vecs = sb("vecs", [P, CB, WIDTH + 3])
        wr = sb("wr", [P, DC, GROUPS + EXPERTS])
        rb = sb("rb", [P, GROUPS + EXPERTS])
        eps = sb("eps", [P, 1])
        sq = sb("sq", [P, 4, 8])
        rs = sb("rs", [P, 4, 8])
        st = sb("st", [P, 2, TILES, 8])
        mv = sb("mv", [P, 2, TILES, 2])
        lr = sb("lr", [P, 2, 8])
        lg = sb("lg", [P, TILES, GROUPS + EXPERTS])
        r1 = sb("r1", [P, 16, TILES])
        rev = sb("rev", [P, GROUPS])
        base = sb("base", [P, EXPERTS])
        pos = sb("pos", [P, TILES, 2], U32)
        pays = sb("pays", [P, TILES, 2, 2], U32)
        lists = sb("lists", [P, EXPERTS, 2], U32)
        gidx = sb("gidx", [P, 1], U32)
        sidx = sb("sidx", [P, 1], U32)
        token = sb("token", [1, 3])
        oidx = sb("oidx", [P, 2], U32)
        wl = sb("wl", [1, 3, 4 * EXPERTS])
        codes = sb("codes", [1, 2, 4 * EXPERTS])
        jobs = sb("jobs", [1, 2 * OVERFLOW_MAX + 1])
        jobs_i = sb("jobs_i", [1, 2 * OVERFLOW_MAX + 1], U32)
        pair = [ctx.enter_context(nc.psum_tensor(f"pair{i}", [P, 2 * 512], F32)) for i in range(4)]
        bank = [pair[i // 2][:, i % 2 * 512:(i % 2 + 1) * 512] for i in range(8)]

        normed = nc.dram_tensor("normed", (TOKENS, D), F32, kind="Internal").ap()
        pairs = nc.dram_tensor("pairs", (2 * TOKENS, D), F32, kind="Internal").ap()
        slots = nc.dram_tensor("slots", (EXPERTS * CAP, 2), U32, kind="Internal").ap()

        H = h[:, :].rearrange("p (t d) -> p t d", t=TILES)
        V = h[:, 0:TILES * C].rearrange("p (t c) -> p t c", t=TILES)
        U = h[:, TILES * C:TILES * C + CB * TOKENS].rearrange("p (b n) -> p b n", b=CB)
        G = conv[:, 0:CB * GROW].rearrange("p (b n) -> p b n", b=CB)
        A = conv[:, CB * GROW:].rearrange("p (b n) -> p b n", b=CB)
        PP = conv[:, 0:TILES * D].rearrange("p (t d) -> p t d", t=TILES)
        tap_rows = two[:, 0:2 * SEQ].rearrange("p (i n) -> p i n", i=2)
        sam_rows = two[:, 0:SEQS * DEC_SEQ * WIDTH]
        GSAM = G[:, :, GP:].rearrange("p b (s k) -> p b s k", s=DEC_BATCH)
        WS = ws[:, 0:HEADS * P].rearrange("p (h n) -> p h n", h=HEADS)
        WSS = ws[:, HEADS * P:].rearrange("p (h n) -> p h n", h=HEADS)
        PN = ws[:, 0:TILES * PLE].rearrange("p (t d) -> p t d", t=TILES)
        ahi = act_hi[:, :].rearrange("p (c n) -> p c n", c=DC)
        alo = act_lo[:, :].rearrange("p (c n) -> p c n", c=DC)
        X_AT, HT_AT, P_AT = 0, DC * P, DC * P + CB * P
        xhi, xlo = (s[:, X_AT:HT_AT].rearrange("p (c n) -> p c n", c=DC) for s in (act_hi, act_lo))
        thi, tlo = (s[:, HT_AT:P_AT].rearrange("p (c n) -> p c n", c=CB) for s in (act_hi, act_lo))
        phi, plo = (s[:, P_AT:P_AT + 2 * TOKENS].rearrange("p (c n) -> p c n", c=2) for s in (act_hi, act_lo))
        xg = two[:, 0:D]
        res = two[:, D:2 * D]
        stn = two[:, 0:2 * C].rearrange("p (i c) -> p i c", i=2)
        SROWS = DEC_BATCH * HIST // 2
        vrow = two[:, 2 * C:3 * C]
        NV = WIDTH + 3
        wssn = two[:, 3 * C:4 * C].rearrange("p (h n) -> p h n", h=HEADS)
        wsn = wide[:, :].rearrange("p (h n) -> p h n", h=HEADS)
        lng, lnb = work[:, 0:C], work[:, C:2 * C]
        sg = gain[:, 0:TOKENS]
        fresh = gain[:, TOKENS:TOKENS + CB * SAMPLE].rearrange("p (b n) -> p b n", b=CB)
        silu, hid = work[:, 0:DE], work[:, DE:2 * DE]
        BS = 64
        bs = two[BS:BS + 1, D:2 * D]
        r16 = conv[:, TILES * D:TILES * D + 6 * TILES * EXPERTS].rearrange("p (a t e) -> p a t e", a=6, t=TILES)
        r4 = ws[:, TILES * PLE:TILES * (PLE + 8 * GROUPS)].rearrange("p (a t g) -> p a t g", a=8, t=TILES)
        wl8 = wide[0:1, :].rearrange("p (q j n) -> p q j n", q=2, j=OVERFLOW_MAX)
        empty = conv[:, TILES * D:TILES * D + WORD_COLS].bitcast(U32)

        x_in = [sem(f"x_in{t}") for t in range(TILES)]
        gain_in = sem("gain_in")
        ln_in = sem("ln_in")
        ws_in = sem("ws_in")
        rows_in = sem("rows_in")
        small_in = sem("small_in")
        raw_in = [sem(f"raw_in{i}") for i in range(RAW)]
        hi_done = sem("hi_done")
        lo_pool = sem("lo_pool")
        lo_dve = sem("lo_dve")
        pe_unit = sem("pe_unit")
        const = sem("const")
        sq_done = sem("sq_done")
        root_done = sem("root_done")
        var_done = sem("var_done")
        sd_done = sem("sd_done")
        norm_done = sem("norm_done")
        xt_ps = sem("xt_ps")
        xt_hi = sem("xt_hi")
        xt_lo = sem("xt_lo")
        setup_ps = sem("setup_ps")
        setup_sb = sem("setup_sb")
        masked = sem("masked")
        z_ps = sem("z_ps")
        sig_done = sem("sig_done")
        glu_done = sem("glu_done")
        acc = sem("acc")
        tap_first = sem("tap_first")
        tap_mul = sem("tap_mul")
        tap_add = sem("tap_add")
        sam_mul = sem("sam_mul")
        sam_sum = sem("sam_sum")
        sam_acc = sem("sam_acc")
        v_ps = sem("v_ps")
        v_gelu = sem("v_gelu")
        u_ps = sem("u_ps")
        u_gelu = sem("u_gelu")
        v_norm = sem("v_norm")
        v_scaled = sem("v_scaled")
        v_ready = sem("v_ready")
        ct_ps = sem("ct_ps")
        ct_norm = sem("ct_norm")
        cc_ps = sem("cc_ps")
        ya_silu = sem("ya_silu")
        ya_hi = sem("ya_hi")
        ya_lo = sem("ya_lo")
        mix_ps = sem("mix_ps")
        yb_mul = sem("yb_mul")
        yb_hi = sem("yb_hi")
        yb_lo = sem("yb_lo")
        x_again = sem("x_again")
        fresh_done = sem("fresh_done")
        state_ps = sem("state_ps")
        state_sb = sem("state_sb")
        o_ps = sem("o_ps")
        o_add = sem("o_add")
        normed_out = [sem(f"normed_out{i}") for i in range(2)]
        rt_ps = sem("rt_ps")
        rt_sb = sem("rt_sb")
        r_ps = sem("r_ps")
        lg_sb = sem("lg_sb")
        p_in = sem("p_in")
        pt_ps = sem("pt_ps")
        pt_hi = sem("pt_hi")
        pt_lo = sem("pt_lo")
        pp_ps = sem("pp_ps")
        pp_sb = sem("pp_sb")
        arg_done = sem("arg_done")
        exp_done = sem("exp_done")
        onehot = sem("onehot")
        rank_ps = sem("rank_ps")
        slot_at = sem("slot_at")
        slots_clear = sem("slots_clear")
        filler_set = sem("filler_set")
        slots_out = sem("slots_out")
        lists_in = sem("lists_in")
        gidx_set = sem("gidx_set")
        sidx_set = sem("sidx_set")
        gathered = sem("gathered")
        g_ps = sem("g_ps")
        g_hi = sem("g_hi")
        g_lo = sem("g_lo")
        silu_done = sem("silu_done")
        hid_done = sem("hid_done")
        t_ps = sem("t_ps")
        t_hi = sem("t_hi")
        t_lo = sem("t_lo")
        res_act = sem("res_act")
        res_dve = sem("res_dve")
        scattered = sem("scattered")
        jobs_done = sem("jobs_done")
        v_idx = sem("v_idx")
        v_w = [sem(f"v_w{i}") for i in range(3)]
        v_in = sem("v_in")
        v_gps = sem("v_gps")
        v_gsb = sem("v_gsb")
        v_gu = sem("v_gu")
        v_silu = sem("v_silu")
        v_hid = sem("v_hid")
        v_tps = sem("v_tps")
        v_tsb = sem("v_tsb")
        v_dps = sem("v_dps")
        v_res = sem("v_res")
        v_out = sem("v_out")
        v_free = sem("v_free")
        pairs_full = sem("pairs_full")
        pair_in = [sem(f"pair_in{i}") for i in range(2)]
        pair_one = sem("pair_one")
        pair_two = sem("pair_two")
        pair_add = sem("pair_add")
        s_ps = sem("s_ps")
        s_sig = sem("s_sig")
        s_mul = sem("s_mul")
        s_add = sem("s_add")
        y_sb = sem("y_sb")
        y_out = [sem(f"y_out{i}") for i in range(2)]
        store = sem("store")
        dve = sem("dve")
        block = ctx.enter_context(nc.Block())

        def windows(b, q):
            new = GSAM[:, b, q * SEQS:(q + 1) * SEQS, 0:DEC_SEQ]
            return bass.AP(tensor=new.tensor, offset=new.offset, ap=[*new.ap, [1, WIDTH]])

        def unit_source(n, d=0):
            def cols(w, at):
                return w[0, :, at:at + UC].rearrange("(c p) n -> p c n", p=P)
            if n < N_OUT:
                return cols(a["w_in"], Z_COLS[n])
            if n < N_PROJ:
                return cols(a["w_out"], (n - N_OUT) * UC)
            if n == N_PROJ:
                return a["w_ple_proj"][0].rearrange("(c p) n -> p c n", p=P)
            if n >= N_GATE:
                return cols(a["w_ple_gate"], (n - N_GATE) * UC)
            k, e = (n - N_MOE, 0) if n < N_STEP else ((n - N_STEP) % 6, 1 + (n - N_STEP) // 6)
            if n >= N_STEP + 6 * (EXPERTS - 1):
                k, e = 4 + (n - N_STEP - 6 * (EXPERTS - 1)), EXPERTS
            e = e + d
            if k < 4:
                w = a["w_exp_gate"] if k < 2 else a["w_exp_up"]
                w = w[0].rearrange("e (c p) n -> (e c) p n", p=P)
                at = e * DC + (k % 2) * (DC // 2)
                return w[bass.ds(at, DC // 2)].rearrange("c p n -> p c n")
            w = a["w_exp_down"][0].rearrange("e (c p) n -> (e c) p n", p=P)
            at = (e - 1) * CB + (k - 4) * 2
            return w[bass.ds(at, 2)].rearrange("c p n -> p c n")

        def wait_all(eng, *waits):
            waits = [(signal, value if isinstance(value, int) else eng.to_reg(value)) for signal, value in waits]
            eng.wait_ge(x_in[0], 16)
            for signal, value in waits:
                eng.wait_ge(signal, value)

        def used(n):
            if n < 4:
                return z_ps, 4 * (n // 2) + n % 2 + 3
            if n < 6:
                return v_ps, TILES * (n - 3)
            if n < N_OUT:
                return u_ps, 2 * (n - 5)
            if n < N_PROJ:
                return o_ps, TILES * (n - N_OUT + 1)
            if n == N_PROJ:
                return pp_ps, TILES
            if n < N_GATE:
                return pe_unit, n - N_MOE + 1
            return s_ps, 3 * TILES - 2 + n - N_GATE

        def wait_used(eng, n, d=0):
            signal, value = used(n)
            eng.wait_ge(signal, value + 6 * d)

        def step_unit(e0, k):
            return N_STEP + 6 * (e0 - 1) + k

        @block.sync
        def _(sp):
            def load_unit(n, d=0):
                if n >= RAW:
                    done = n - RAW + 1 + 6 * d
                    low = [(lo_dve, n - RAW - N_MOE + 1 + 6 * d)] if n - RAW >= N_MOE else []
                    wait_all(sp, (hi_done, done), (lo_pool, done), *low)
                src = unit_source(n, d)
                sp.dma_start(raw[:, n % RAW, :].rearrange("p (c n) -> p c n", c=src.shape[1]), src)\
                  .then_inc(raw_in[n % RAW], 16)

            for t in range(TILES):
                x = a["x_prompt"][0, t * P:(t + 1) * P] if t < TILES - 1 else a["x_sample"].rearrange("b s d -> (b s) d")
                sp.dma_start(H[0:rows(t), t, :], x).then_inc(x_in[t], 16)
            for n in range(3):
                load_unit(n)
            sp.dma_start(vrow[0:WIDTH, :], a["conv_w"][0]).then_inc(rows_in, 16)
            for i, name in enumerate(("conv_b", "conv_ln_g", "conv_ln_b")):
                sp.dma_start(vrow[WIDTH + i:WIDTH + i + 1, :], a[name]).then_inc(rows_in, 16)
            states = a["state_conv"][0].rearrange("s k c -> (s k) c")
            for i in range(2):
                sp.dma_start(stn[0:SROWS, i, :], states[i * SROWS:(i + 1) * SROWS]).then_inc(rows_in, 16)
            for n in range(3, RAW):
                load_unit(n)
            sp.dma_start(out["state_conv_sample"][0, :, 0:HIST - DEC_SEQ],
                         a["state_conv"][0, :, DEC_SEQ:HIST]).then_inc(store, 16)
            for n in range(RAW, N_OUT):
                load_unit(n)
            for n in range(N_OUT, N_OUT + 3):
                load_unit(n)
            sp.wait_ge(v_ready, TILES)
            sp.dma_start(out["state_gmlp_v_sample"][0].rearrange("b s c -> (b s) c"),
                         V[0:SAMPLE, TILES - 1, :]).then_inc(store, 16)
            sp.wait_ge(yb_mul, TILES)
            sp.wait_ge(store, 32)
            for t in range(TILES):
                x = a["x_prompt"][0, t * P:(t + 1) * P] if t < TILES - 1 else a["x_sample"].rearrange("b s d -> (b s) d")
                sp.dma_start(H[0:rows(t), t, :], x).then_inc(x_again, 16)
            sp.wait_ge(state_sb, 1)
            sp.dma_start(out["state_conv_prompt"][0, 0], work[0:HIST, 0:C]).then_inc(store, 16)
            sp.wait_ge(state_sb, 2)
            for s in range(DEC_BATCH):
                sp.dma_start(out["state_conv_sample"][0, s, HIST - DEC_SEQ:HIST],
                             work[s * DEC_SEQ:(s + 1) * DEC_SEQ, C:2 * C]).then_inc(store, 16)
            for n in range(N_OUT + 3, N_STEP):
                load_unit(n)
            for k in range(6):
                if k == 2:
                    sp.wait_ge(gathered, 16)
                load_unit(step_unit(1, k))
            with sp.Fori(0, EXPERTS - 2) as d:
                for k in range(6):
                    load_unit(step_unit(2, k), d)
            for n in range(N_GATE - 2, N_GATE):
                load_unit(n)

            sp.wait_ge(jobs_done, 1)
            jobs_n = sp.value_load(jobs_i[0:1, 2 * OVERFLOW_MAX:], min_val=0, max_val=OVERFLOW_MAX)
            with sp.If(jobs_n > 0):
                with sp.Fori(0, jobs_n) as j:
                    e = sp.value_load(jobs_i[0:1, bass.ds(j, 1)], min_val=0, max_val=EXPERTS - 1)
                    at = sp.value_load(jobs_i[0:1, bass.ds(j + OVERFLOW_MAX, 1)], min_val=0, max_val=EXPERTS * CAP - P)
                    wait_all(sp, (v_free, j + 1))
                    sp.dma_start(oidx[:, :], slots[bass.ds(at, P), :]).then_inc(v_idx, 16)
                    for i, name in enumerate(("w_exp_gate", "w_exp_up", "w_exp_down")):
                        c = CB // 2 if i == 2 else DC // 2
                        src = a[name][0].rearrange("e (c p) n -> (e c) p n", p=P)
                        for k in range(2):
                            n = N_GATE - RAW + 2 * i + k
                            sp.wait_ge(hi_done, n + 1)
                            sp.wait_ge(lo_pool, n + 1)
                            sp.wait_ge(lo_dve, n - N_MOE + 1)
                            sp.dma_start(raw[:, n % RAW, :].rearrange("p (c n) -> p c n", c=c),
                                         src[bass.ds(e * 2 * c + k * c, c)].rearrange("c p n -> p c n")).then_inc(v_w[i], 16)
                wait_all(sp, (v_gu, jobs_n))
            for n in range(N_GATE, N_UNITS):
                load_unit(n)
            sp.wait_ge(pairs_full, 1)
            for t in range(TILES):
                if t >= 2:
                    sp.wait_ge(pair_add, t - 1)
                sp.dma_start(raw[0:rows(t), PAIR_SLOTS[t % 2], :],
                             pairs[2 * P * t:2 * (P * t + rows(t)), :].rearrange("(n k) d -> n (k d)", k=2))\
                  .then_inc(pair_in[t % 2], 16)
            for t in range(TILES):
                sp.wait_ge(y_sb, t + 1)
                y = out["y_prompt"][0, t * P:(t + 1) * P] if t < TILES - 1 else out["y_sample"].rearrange("b s d -> (b s) d")
                sp.dma_start(y, two[0:rows(t), (t % 2) * D:(t % 2 + 1) * D]).then_inc(y_out[t % 2], 16)
            for i in range(2):
                sp.wait_ge(y_out[i], 16 * ((TILES + 1 - i) // 2))
            sp.wait_ge(store, 16 * (3 + DEC_BATCH))

        @block.gpsimd
        def _(g):
            own = [0]

            def made(ins):
                ins.then_inc(const, 1)
                own[0] += 1

            def link(ins):
                made(ins)
                g.wait_ge(const, own[0])

            def select(t, op, fill, start, pattern, mult):
                return nc.gpsimd.affine_select(out=t, in_=t, compare_op=op, fill=fill, base=start,
                                               pattern=pattern, channel_multiplier=mult)

            link(nc.gpsimd.memset(ident[:, :], 0.0))
            made(select(ident[:, :], ALU.not_equal, 1.0, 0, [[-1, P]], 1))
            made(nc.gpsimd.memset(sq[:, :, :], 1.0))
            made(nc.gpsimd.memset(eps[:, :], EPS))
            made(nc.gpsimd.memset(G[:, :, 0:HIST], 0.0))
            made(nc.gpsimd.memset(mv[:, :, :, :], 1.0))
            made(nc.gpsimd.memset(ones[:, :], 1.0))
            link(nc.gpsimd.memset(wssn[0:SAMPLE], 0.0))
            for s in range(DEC_BATCH):
                r = slice(s * DEC_SEQ, (s + 1) * DEC_SEQ)
                nc.gpsimd.dma_start(wssn[r, :, r], a["w_s"][0, :, 0:DEC_SEQ, 0:DEC_SEQ].rearrange("h i j -> i h j"))\
                  .then_inc(ws_in, 16)
            nc.gpsimd.dma_start(wsn, a["w_s"][0].rearrange("h i j -> i h j")).then_inc(ws_in, 16)
            nc.gpsimd.memset(empty, NOBODY).then_inc(filler_set, 1)
            g.wait_ge(filler_set, 1)
            nc.gpsimd.dma_start(slots.rearrange("(p s) k -> p (s k)", p=P), empty).then_inc(slots_clear, 16)

            def split_low(n, d=0):
                share = LOW_POOL if n >= N_MOE else UNIT
                g.wait_ge(hi_done, n + 1 + 6 * d)
                if n >= SPLIT:
                    wait_used(g, n - SPLIT, d)
                s = slice(UNIT - share, UNIT)
                nc.gpsimd.tensor_tensor(lo[:, n % SPLIT, s], raw[:, n % RAW, s],
                                        hi[:, n % SPLIT, s].bitcast(F32), ALU.subtract).then_inc(lo_pool, 1)

            for n in range(SPLIT):
                split_low(n)
            g.wait_ge(ws_in, 16 * (DEC_BATCH + 1))
            select(wsn, ALU.is_ge, 0.0, 0, [[0, HEADS], [-1, P]], 1).then_inc(masked, 1)
            select(wssn[0:SAMPLE], ALU.is_ge, 0.0, 0, [[0, HEADS], [-1, SAMPLE]], 1).then_inc(masked, 1)
            link(nc.gpsimd.memset(before[:, :], 1.0))
            made(select(before[:, :], ALU.is_gt, 0.0, 0, [[1, P]], -1))
            made(nc.gpsimd.iota(rev[:, :], [[-1, GROUPS]], base=GROUPS, channel_multiplier=0,
                                allow_small_or_imprecise_dtypes=True))
            made(nc.gpsimd.iota(base[:, :], [[CAP, EXPERTS]], base=0, channel_multiplier=0,
                                allow_small_or_imprecise_dtypes=True))
            for t in range(TILES):
                made(nc.gpsimd.iota(pays[:, t, :, 0], [[0, 2]], base=P * t, channel_multiplier=1))
                made(nc.gpsimd.iota(pays[:, t, :, 1], [[1, 2]], base=2 * P * t, channel_multiplier=2))
            made(nc.gpsimd.iota(codes[:, 0, :], [[0, 4], [1, EXPERTS]], base=0, channel_multiplier=0,
                                allow_small_or_imprecise_dtypes=True))
            made(nc.gpsimd.iota(codes[:, 1, :], [[P, 4], [CAP, EXPERTS]], base=P, channel_multiplier=0,
                                allow_small_or_imprecise_dtypes=True))
            made(nc.gpsimd.memset(wl[:, 2, :], 0.0))
            made(nc.gpsimd.memset(lg[:, :, :], 0.0))
            assert own[0] == N_CONST

            def tap_chunk(c):
                first = 1 + TAP_CHUNK * c

                def add(k, i):
                    g.wait_ge(tap_mul, k + i)
                    nc.gpsimd.tensor_tensor(A[:, TAP_BLOCK, 0:SEQ], A[:, TAP_BLOCK, 0:SEQ], tap_rows[:, i, :],
                                            ALU.add).then_inc(tap_add, 1)

                if c >= TAP_CHUNKS:
                    k = WIDTH - 2 * (TAP_PAIRS - (c - TAP_CHUNKS))
                    for i in range(2):
                        g.wait_ge(tap_add, k + i - 1)
                        add(k, i)
                    return
                if c == 0:
                    g.wait_ge(tap_first, 1)
                    add(1, 0)
                    g.wait_ge(tap_add, 1)
                    add(1, 1)
                    first = 3
                with g.Fori(first, 1 + TAP_CHUNK * (c + 1), 2) as k:
                    for i in range(2):
                        g.wait_ge(tap_add, k + i - 1)
                        add(k, i)

            split_low(SPLIT)
            for b in range(1, CB):
                split_low(SPLIT + b)
                if b <= TAP_CHUNKS:
                    tap_chunk(b - 1)
            for i in range(TAP_PAIRS):
                if i == TILES - 1:
                    split_low(N_OUT - 1)
                tap_chunk(TAP_CHUNKS + i)
            def v_affine(step):
                t = step // 2
                r = rows(t)
                if step % 2 == 0:
                    g.wait_ge(v_norm, t + 1)
                    nc.gpsimd.tensor_tensor(V[0:r, t, :], V[0:r, t, :], lng[0:r], ALU.mult).then_inc(v_scaled, 1)
                else:
                    g.wait_ge(v_scaled, t + 1)
                    nc.gpsimd.tensor_tensor(V[0:r, t, :], V[0:r, t, :], lnb[0:r], ALU.add).then_inc(v_ready, 1)

            g.wait_ge(tap_add, WIDTH - 1)
            g.wait_ge(ln_in, 32)
            parts = CB * DEC_BATCH // SEQS
            for q in range(parts):
                b, i = divmod(q, DEC_BATCH // SEQS)
                g.wait_ge(glu_done, 3 * b + 3)
                if q >= 1:
                    g.wait_ge(sam_sum, q)
                nc.gpsimd.tensor_tensor(sam_rows.rearrange("p (s n k) -> p s n k", s=SEQS, n=DEC_SEQ), windows(b, i),
                                        vecs[:, b, 0:WIDTH].unsqueeze(1).unsqueeze(1)
                                        .to_broadcast([P, SEQS, DEC_SEQ, WIDTH]), ALU.mult).then_inc(sam_mul, 1)
                v_affine(q)
            for step in range(parts, 2 * TILES):
                v_affine(step)
            for n in range(N_OUT, N_MOE + 2):
                split_low(n)
            g.wait_ge(rt_ps, TILES)
            for i in range(2):
                g.wait_ge(normed_out[i], 16 * ((TILES + 1 - i) // 2))
            nc.gpsimd.memset(xg, 0.0).then_inc(gidx_set, 1)
            g.wait_ge(slots_clear, 16)
            g.wait_ge(slot_at, 1)
            for t in range(TILES):
                for k in range(2):
                    nc.gpsimd.indirect_dma_start(
                        slots, bass.IndirectOffsetOnAxis(pos[0:rows(t), t, k:k + 1], 0),
                        pays[0:rows(t), t, k, :], None).then_inc(slots_out, 16)

            last_token = g.to_reg(TOKENS - 1)
            last_pair = g.to_reg(2 * TOKENS - 1)

            def gather(e0, d=0):
                if e0 > 0:
                    g.wait_ge(gathered, 16 * (e0 + d))
                    g.wait_ge(g_ps, e0 + d)
                nc.gpsimd.tensor_copy(gidx[:, :], lists[:, bass.ds(e0 + d, 1), 0]).then_inc(gidx_set, 1)
                wait_all(g, (gidx_set, e0 + 2 + d))
                nc.gpsimd.indirect_dma_start(xg, None, normed, bass.IndirectOffsetOnAxis(gidx[:, :], 0),
                                             bounds_check=last_token, oob_is_err=False).then_inc(gathered, 16)

            def scatter(e0, d=0):
                if e0 > 0:
                    g.wait_ge(scattered, 16 * (e0 + d))
                nc.gpsimd.tensor_copy(sidx[:, :], lists[:, bass.ds(e0 + d, 1), 1]).then_inc(sidx_set, 1)
                wait_all(g, (sidx_set, e0 + 1 + d), (res_act, e0 + 1 + d), (res_dve, e0 + 1 + d))
                nc.gpsimd.indirect_dma_start(pairs, bass.IndirectOffsetOnAxis(sidx[:, :], 0), res, None,
                                             bounds_check=last_pair, oob_is_err=False).then_inc(scattered, 16)

            def step(e0, d=0):
                if e0 < EXPERTS - 1:
                    gather(e0 + 1, d)
                if e0 == 0:
                    for n in range(N_MOE + 2, N_STEP + 2):
                        split_low(n)
                    return
                for k in range(2, 8):
                    split_low(step_unit(e0, k), d)
                scatter(e0 - 1, d)

            g.wait_ge(lists_in, 16)
            g.wait_ge(gidx_set, 1)
            gather(0)
            step(0)
            step(1)
            with g.Fori(0, EXPERTS - 3) as d:
                step(2, d)
            nc.gpsimd.memset(token[:, 2:3], 0.0).then_inc(v_free, 1)
            for k in range(2, 8):
                split_low(step_unit(EXPERTS - 1, k))
            scatter(EXPERTS - 2)

            def overflow_gather(j):
                wait_all(g, (v_idx, 16 * j + 16))
                nc.gpsimd.indirect_dma_start(xg, None, normed, bass.IndirectOffsetOnAxis(oidx[:, 0:1], 0),
                                             bounds_check=last_token, oob_is_err=False).then_inc(v_in, 16)

            g.wait_ge(jobs_done, 1)
            jobs_n = g.value_load(jobs_i[0:1, 2 * OVERFLOW_MAX:], min_val=0, max_val=OVERFLOW_MAX)
            with g.If(jobs_n > 0):
                g.wait_ge(gathered, 16 * EXPERTS)
                g.wait_ge(g_ps, EXPERTS)
                overflow_gather(0)
            scatter(EXPERTS - 1)
            with g.If(jobs_n > 0):
                with g.Fori(0, jobs_n) as j:
                    wait_all(g, (v_res, j + 1))
                    nc.gpsimd.indirect_dma_start(pairs, bass.IndirectOffsetOnAxis(oidx[:, 1:2], 0), res, None,
                                                 bounds_check=last_pair, oob_is_err=False).then_inc(v_out, 16)
                    wait_all(g, (v_out, 16 * j + 16))
                    nc.gpsimd.memset(token[:, 0:1], 0.0).then_inc(v_free, 1)
                    with g.If(jobs_n > j + 1):
                        overflow_gather(j + 1)
            g.wait_ge(scattered, 16 * EXPERTS)
            nc.gpsimd.memset(token[:, 1:2], 0.0).then_inc(pairs_full, 1)
            for n in range(N_GATE, N_GATE + SPLIT):
                split_low(n)
            for t in range(TILES):
                r = rows(t)
                g.wait_ge(pair_one, t + 1)
                g.wait_ge(pair_two, t + 1)
                nc.gpsimd.tensor_tensor(H[0:r, t, :], H[0:r, t, :], raw[0:r, PAIR_SLOTS[t % 2], D:2 * D],
                                        ALU.add).then_inc(pair_add, 1)
            split_low(N_GATE + SPLIT)

        @block.scalar
        def _(act):
            def copy(out_, in_):
                return nc.scalar.activation(out_, in_, ACT.Copy)

            def load_gain(name):
                src = a[name] if len(a[name].shape) == 2 else a[name].rearrange("(o d) -> o d", o=1)
                act.dma_start(gain[:, :], src.to_broadcast([P, D])).then_inc(gain_in, 16)

            def split_high(n, d=0):
                act.wait_ge(raw_in[n % RAW], 16 * (n // RAW + 1) + 16 * d)
                if n >= SPLIT:
                    wait_used(act, n - SPLIT, d)
                copy(hi[:, n % SPLIT, :], raw[:, n % RAW, :]).then_inc(hi_done, 1)

            def square(t, w):
                nc.scalar.activation(work[0:rows(t), :], H[0:rows(t), t, :], ACT.Square, scale=1.0 / D ** 0.5,
                                     accum_out=sq[0:rows(t), w, t:t + 1]).then_inc(sq_done, 1)

            def root(w, t):
                act.wait_ge(sq_done, TILES * w + t + 1)
                nc.scalar.activation(rs[0:rows(t), w, t:t + 1], sq[0:rows(t), w, t:t + 1], ACT.Sqrt,
                                     bias=eps[0:rows(t), :]).then_inc(root_done, 1)

            def deviation(which):
                act.wait_ge(var_done, which + 1)
                nc.scalar.activation(lr[:, which, 0:TILES], lr[:, which, 0:TILES], ACT.Sqrt, bias=eps[:, :])\
                    .then_inc(sd_done, 1)

            def normed_high(t, w):
                r = rows(t)
                act.wait_ge(xt_ps, (0 if w == MIX else TILES) + t + 1)
                copy(ahi[:, :, t * P:t * P + r], pair[t % 2][:, :].rearrange("p (c n) -> p c n", c=DC)[:, :, 0:r])\
                    .then_inc(xt_hi, 1)

            load_gain("norm_mix_g")
            act.wait_ge(const, N_CONST_SQ)
            for t in range(TILES):
                act.wait_ge(x_in[t], 16)
                square(t, MIX)
                root(MIX, t)
                if t == 3:
                    normed_high(0, MIX)
            split_high(0)
            for t in range(1, TILES):
                normed_high(t, MIX)
                if t % 2:
                    split_high((t + 1) // 2)
            act.wait_ge(setup_ps, 1)
            copy(vecs[:, :, :], bank[4].rearrange("p (b n) -> p b n", b=CB)[:, :, 0:NV]).then_inc(setup_sb, 1)
            for i in range(2):
                act.wait_ge(setup_ps, 2 + i)
                for b in range(CB):
                    copy(GSAM[:, b, 4 * i:4 * i + 4, 0:HIST],
                         bank[5 + i][:, b * P:b * P + SROWS].rearrange("p (s k) -> p s k", k=HIST)).then_inc(setup_sb, 1)

            act.dma_start(bs, a["b_s"].rearrange("o h n -> o (h n)")).then_inc(small_in, 16)
            act.dma_start(wr[:, :, 0:GROUPS], a["w_router_group"][0].rearrange("(c p) n -> p c n", p=P)).then_inc(small_in, 16)
            act.dma_start(wr[:, :, GROUPS:], a["w_router_expert"][0].rearrange("(c p) n -> p c n", p=P)).then_inc(small_in, 16)
            act.dma_start(rb[:, 0:GROUPS], a["b_router_group"].to_broadcast([P, GROUPS])).then_inc(small_in, 16)
            act.dma_start(rb[:, GROUPS:], a["b_router_expert"].to_broadcast([P, EXPERTS])).then_inc(small_in, 16)
            act.wait_ge(sq_done, TILES)
            act.dma_start(lng, a["gmlp_ln_g"].to_broadcast([P, C])).then_inc(ln_in, 16)
            act.dma_start(lnb, a["gmlp_ln_b"].to_broadcast([P, C])).then_inc(ln_in, 16)
            def sigmoid(b):
                act.wait_ge(z_ps, 2 * b + 2)
                if b == 0:
                    act.wait_ge(norm_done, TILES)
                else:
                    act.wait_ge(glu_done, 3 * b)
                nc.scalar.activation(sg.rearrange("p (s n) -> p s n", s=2),
                                     pair[2 * (b % 2) + 1][:, :].rearrange("p (s n) -> p s n", s=2)[:, :, 0:HALF],
                                     ACT.Sigmoid).then_inc(sig_done, 1)

            def tap(k, i):
                at = k + i
                nc.scalar.activation(tap_rows[:, i, :], G[:, TAP_BLOCK, bass.ds(at, SEQ)], ACT.Copy,
                                     scale=vecs[:, TAP_BLOCK, bass.ds(at, 1)]).then_inc(tap_mul, 1)

            def tap_chunk(c):
                first = 1 + TAP_CHUNK * c
                if c == 0:
                    act.wait_ge(glu_done, 3 * TAP_BLOCK + 3)
                    nc.scalar.activation(A[:, TAP_BLOCK, 0:SEQ], G[:, TAP_BLOCK, 0:SEQ], ACT.Identity,
                                         scale=vecs[:, TAP_BLOCK, 0:1], bias=vecs[:, TAP_BLOCK, WIDTH:WIDTH + 1])\
                        .then_inc(tap_first, 1)
                    tap(1, 0)
                    tap(1, 1)
                    first = 3
                with act.Fori(first, 1 + TAP_CHUNK * (c + 1), 2) as k:
                    for i in range(2):
                        act.wait_ge(tap_add, k + i - 2)
                        tap(k, i)

            for b in range(CB):
                sigmoid(b)
                split_high(SPLIT + b)
                if 1 <= b <= TAP_CHUNKS:
                    tap_chunk(b - 1)
            for q in range(2 * TILES):
                i, t = divmod(q, TILES)
                if 1 <= q <= TAP_PAIRS:
                    for i_tap in range(2):
                        k = WIDTH - 2 * (TAP_PAIRS - q + 1)
                        act.wait_ge(tap_add, k + i_tap - 2)
                        tap(k, i_tap)
                act.wait_ge(v_ps, q + 1)
                nc.scalar.activation(V[0:rows(t), t, i * UC:(i + 1) * UC], bank[q % 4][0:rows(t), 0:UC],
                                     ACT.Gelu_apprx_tanh).then_inc(v_gelu, 1)
                if t == TILES - 1:
                    split_high(7 + i)
            deviation(0)
            for b in range(CB):
                act.wait_ge(u_ps, b + 1)
                nc.scalar.activation(U[:, b, :].rearrange("p (s n) -> p s n", s=2),
                                     pair[2 + b % 2][:, :].rearrange("p (s n) -> p s n", s=2)[:, :, 0:HALF],
                                     ACT.Gelu_apprx_tanh).then_inc(u_gelu, 1)
                if b % 2:
                    split_high(9 + b // 2)
            act.wait_ge(glu_done, 3 * CB)
            copy(fresh.rearrange("p b (s k) -> p b s k", k=DEC_SEQ), GSAM[:, :, :, HIST:]).then_inc(fresh_done, 1)
            act.wait_ge(setup_ps, 4)
            copy(WS, pair[0][:, :].rearrange("p (h n) -> p h n", h=HEADS)).then_inc(setup_sb, 1)
            act.wait_ge(setup_ps, 5)
            copy(WSS[0:SAMPLE], bank[2][0:SAMPLE, :].rearrange("p (h n) -> p h n", h=HEADS)).then_inc(setup_sb, 1)
            deviation(1)
            for t in range(TILES):
                act.wait_ge(yb_mul, t + 1)
                copy(ahi[:, CB:, t * P:t * P + rows(t)],
                     two[:, (t % 2) * C:(t % 2 + 1) * C].rearrange("p (b n) -> p b n", b=CB)[:, :, 0:rows(t)])\
                    .then_inc(yb_hi, 1)
            act.wait_ge(mix_ps, TILES)
            for t in range(TILES):
                p = a["p_prompt"][0, 0, t * P:(t + 1) * P] if t < TILES - 1 else a["p_sample"][0].rearrange("b s d -> (b s) d")
                act.dma_start(PN[0:rows(t), t, :], p).then_inc(p_in, 16)
            for t in range(TILES):
                r = rows(t)
                ya = wide[:, (t % 2) * C:(t % 2 + 1) * C].rearrange("p (b n) -> p b n", b=CB)
                act.wait_ge(cc_ps, t + 1)
                if t >= 2:
                    act.wait_ge(ya_lo, t - 1)
                for b in range(CB):
                    nc.scalar.activation(ya[:, b, 0:r], bank[(7, 1)[t % 2]][:, b * P:b * P + r], ACT.Silu,
                                         scale=vecs[:, b, WIDTH + 1:WIDTH + 2], bias=vecs[:, b, WIDTH + 2:WIDTH + 3])\
                        .then_inc(ya_silu, 1)
                act.wait_ge(ya_silu, CB * (t + 1))
                copy(ahi[:, 0:CB, t * P:t * P + r], ya[:, :, 0:r]).then_inc(ya_hi, 1)
            act.wait_ge(state_ps, 1)
            copy(work[0:HIST, 0:C], bank[6][0:HIST, :]).then_inc(state_sb, 1)
            act.wait_ge(state_ps, 2)
            copy(work[0:SAMPLE, C:2 * C], bank[0][0:SAMPLE, :]).then_inc(state_sb, 1)
            load_gain("norm_ffn_g")
            split_high(11)
            split_high(12)
            split_high(13)

            def router_input(t):
                act.wait_ge(norm_done, TILES + t + 1)
                act.dma_start(normed[t * P:t * P + rows(t), :], two[0:rows(t), (t % 2) * D:(t % 2 + 1) * D])\
                   .then_inc(normed_out[t % 2], 16)
                act.wait_ge(rt_ps, t + 1)
                if t > 0:
                    act.wait_ge(r_ps, t)
                copy(wide[:, :].rearrange("p (c n) -> p c n", c=DC)[:, :, 0:rows(t)],
                     pair[(0, 3)[t % 2]][:, :].rearrange("p (c n) -> p c n", c=DC)[:, :, 0:rows(t)]).then_inc(rt_sb, 1)

            act.wait_ge(store, 16 * (3 + DEC_BATCH))
            for t in range(TILES):
                act.wait_ge(o_add, 3 * TILES + t + 1)
                act.wait_ge(sq_done, TILES + t)
                square(t, FFN)
                root(FFN, t)
                if t >= 2:
                    router_input(t - 2)
            act.wait_ge(o_ps, TILES * D // UC)
            for t in range(TILES):
                act.wait_ge(pt_ps, t + 1)
                copy(phi[:, :, t * P:t * P + rows(t)],
                     bank[4 + t % 2][:, 0:2 * P].rearrange("p (c n) -> p c n", c=2)[:, :, 0:rows(t)]).then_inc(pt_hi, 1)
            split_high(14)
            router_input(TILES - 2)
            router_input(TILES - 1)
            load_gain("norm_ple_g")
            for i in range(2):
                act.wait_ge(arg_done, i + 1)
                arg = r4[:, 0, :, :] if i == 0 else r1[:, 2, :]
                nc.scalar.activation(arg, arg, ACT.Exp).then_inc(exp_done, 1)
            for t in range(TILES):
                act.wait_ge(pp_ps, t + 1)
                copy(PP[0:rows(t), t, :], pair[(0, 3)[t % 2]][0:rows(t), :]).then_inc(pp_sb, 1)
            act.wait_ge(slots_out, 16 * 2 * TILES)
            act.dma_start(lists[:, :, :], slots.rearrange("(e s) k -> s e k", s=CAP)[0:P]).then_inc(lists_in, 16)

            def gather_high(e0, d=0):
                act.wait_ge(g_ps, e0 + 1 + d)
                copy(xhi, pair[1][:, :].rearrange("p (c n) -> p c n", c=DC)).then_inc(g_hi, 1)

            def silu_of(e0, d=0):
                wait_used(act, N_MOE + 1 if e0 == 0 else step_unit(e0, 1), d)
                if e0 > 0:
                    act.wait_ge(hid_done, e0 + d)
                nc.scalar.activation(silu, bank[0], ACT.Silu).then_inc(silu_done, 1)

            def hidden_high(e0, d=0):
                act.wait_ge(t_ps, e0 + 1 + d)
                copy(thi, bank[4].rearrange("p (c n) -> p c n", c=CB)).then_inc(t_hi, 1)

            def result(n, e0, d=0):
                wait_used(act, n, d)
                if e0 > 0:
                    act.wait_ge(scattered, 16 * (e0 + d))
                copy(res[:, 0:C], bank[6]).then_inc(res_act, 1)

            def step(e0, d=0):
                if e0 == 0:
                    split_high(N_MOE + 2)
                    split_high(N_MOE + 3)
                    silu_of(0)
                    split_high(N_STEP)
                    gather_high(1)
                    split_high(N_STEP + 1)
                    hidden_high(0)
                    return
                for k in range(2, 5):
                    split_high(step_unit(e0, k), d)
                silu_of(e0, d)
                split_high(step_unit(e0, 5), d)
                if e0 < EXPERTS - 1:
                    gather_high(e0 + 1, d)
                split_high(step_unit(e0, 6), d)
                split_high(step_unit(e0, 7), d)
                hidden_high(e0, d)
                result(step_unit(e0, 5), e0 - 1, d)

            gather_high(0)
            step(0)
            step(1)
            with act.Fori(0, EXPERTS - 3) as d:
                step(2, d)
            step(EXPERTS - 1)
            result(N_GATE - 1, EXPERTS - 1)

            act.wait_ge(jobs_done, 1)
            jobs_n = act.value_load(jobs_i[0:1, 2 * OVERFLOW_MAX:], min_val=0, max_val=OVERFLOW_MAX)
            with act.If(jobs_n > 0):
                act.wait_ge(scattered, 16 * EXPERTS)
                with act.Fori(0, jobs_n) as j:
                    act.wait_ge(v_gps, j + 1)
                    copy(wide[:, :], pair[1][:, :]).then_inc(v_gsb, 1)
                    act.wait_ge(v_gu, j + 1)
                    nc.scalar.activation(silu, bank[0], ACT.Silu).then_inc(v_silu, 1)
                    act.wait_ge(v_tps, j + 1)
                    copy(wide[:, 0:C], bank[4]).then_inc(v_tsb, 1)
                    act.wait_ge(v_dps, j + 1)
                    copy(res, pair[3][:, :]).then_inc(v_res, 1)
            for n in range(N_GATE, N_GATE + SPLIT):
                split_high(n)

            def final_square(t):
                act.wait_ge(s_add, 3 * TILES + t + 1)
                act.wait_ge(sq_done, 3 * TILES + t)
                square(t, FINAL)

            def weigh(t):
                act.wait_ge(pair_in[t % 2], 16 * (t // 2 + 1))
                row = raw[0:rows(t), PAIR_SLOTS[t % 2], D:2 * D]
                nc.scalar.activation(row, row, ACT.Copy, scale=r1[0:rows(t), 8, t:t + 1]).then_inc(pair_two, 1)

            def gate_sigmoid(q, t):
                act.wait_ge(s_ps, q + 1)
                if q >= 4:
                    act.wait_ge(s_add, q - 3)
                nc.scalar.activation(wide[0:rows(t), (q % 4) * UC:(q % 4 + 1) * UC], bank[4 + q % 4][0:rows(t), 0:UC],
                                     ACT.Sigmoid).then_inc(s_sig, 1)

            weigh(0)
            for t in range(TILES):
                if t + 1 < TILES:
                    weigh(t + 1)
                act.wait_ge(pair_add, t + 1)
                act.wait_ge(sq_done, 2 * TILES + t)
                square(t, GATE)
                root(GATE, t)
                if t >= 1:
                    normed_high(t - 1, GATE)
                if t >= 2:
                    for i in range(SPLIT):
                        gate_sigmoid(SPLIT * (t - 2) + i, t - 2)
            normed_high(TILES - 1, GATE)
            act.wait_ge(norm_done, 3 * TILES)
            load_gain("norm_final_g")
            for q, (i, t) in list(enumerate(GATE_ORDER))[SPLIT * (TILES - 2):]:
                if q == 3 * TILES - 1:
                    split_high(N_GATE + SPLIT)
                gate_sigmoid(q, t)
                if q > 3 * TILES:
                    final_square(t - 1)
                if t == TILES - 2 and q > 3 * TILES:
                    for u in range(t):
                        root(FINAL, u)
            root(FINAL, TILES - 2)
            final_square(TILES - 1)
            root(FINAL, TILES - 1)

        @block.vector
        def _(v):
            own = [0]

            def link(ins):
                ins.then_inc(dve, 1)
                own[0] += 1
                v.wait_ge(dve, own[0])

            def inverse_root(w, t):
                v.wait_ge(root_done, TILES * w + t + 1)
                r = rows(t)
                link(nc.vector.reciprocal(rs[0:r, w, t:t + 1], rs[0:r, w, t:t + 1]))

            def apply_norm(t, w, to):
                r = rows(t)
                return nc.vector.scalar_tensor_tensor(out=to[0:r], in0=H[0:r, t, :], scalar=rs[0:r, w, t:t + 1],
                                                      in1=gain[0:r, :], op0=ALU.mult, op1=ALU.mult)

            def normed_low(t, w):
                r = rows(t)
                v.wait_ge(xt_hi, (0 if w == MIX else TILES) + t + 1)
                nc.vector.tensor_tensor(alo[:, :, t * P:t * P + r],
                                        pair[t % 2][:, :].rearrange("p (c n) -> p c n", c=DC)[:, :, 0:r],
                                        ahi[:, :, t * P:t * P + r].bitcast(F32), ALU.subtract).then_inc(xt_lo, 1)

            v.wait_ge(gain_in, 16)
            for t in range(TILES):
                inverse_root(MIX, t)
                apply_norm(t, MIX, H[:, t, :]).then_inc(norm_done, 1)
                if t >= 1:
                    normed_low(t - 1, MIX)
            normed_low(TILES - 1, MIX)

            def glu(b):
                v.wait_ge(sig_done, b + 1)
                val = pair[2 * (b % 2)][:, :].rearrange("p (s n) -> p s n", s=2)
                cut = SEQ - HALF
                nc.vector.tensor_tensor(G[:, b, HIST:HIST + HALF], val[:, 0, 0:HALF], sg[:, 0:HALF],
                                        ALU.mult).then_inc(glu_done, 1)
                nc.vector.tensor_tensor(G[:, b, HIST + HALF:GP], val[:, 1, 0:cut], sg[:, HALF:SEQ],
                                        ALU.mult).then_inc(glu_done, 1)
                nc.vector.tensor_tensor(GSAM[:, b, :, HIST:], val[:, 1, cut:HALF].rearrange("p (s k) -> p s k", k=DEC_SEQ),
                                        sg[:, SEQ:].rearrange("p (s k) -> p s k", k=DEC_SEQ), ALU.mult)\
                    .then_inc(glu_done, 1)

            def first_tap(b):
                v.wait_ge(glu_done, 3 * b + 3)
                w, bias = vecs[:, b, 0:1], vecs[:, b, WIDTH:WIDTH + 1]
                nc.vector.tensor_scalar(A[:, b, 0:SEQ], G[:, b, 0:SEQ], w, bias, ALU.mult, ALU.add).then_inc(acc, 1)

            def taps(b, first, last):
                with v.Fori(first, last) as k:
                    w = vecs[:, b, bass.ds(k, 1)]
                    v.wait_ge(acc, WIDTH * DVE_BLOCKS.index(b) + k)
                    nc.vector.scalar_tensor_tensor(out=A[:, b, 0:SEQ], in0=G[:, b, bass.ds(k, SEQ)], scalar=w,
                                                   in1=A[:, b, 0:SEQ], op0=ALU.mult, op1=ALU.add).then_inc(acc, 1)

            def sample_sum(q):
                b, i = divmod(q, DEC_BATCH // SEQS)
                n = SEQS * DEC_SEQ
                at = A[:, b, SEQ + i * n:SEQ + (i + 1) * n]
                v.wait_ge(sam_mul, q + 1)
                nc.vector.tensor_reduce(at, sam_rows.rearrange("p (n k) -> p n k", k=WIDTH), AX_X, ALU.add)\
                    .then_inc(sam_sum, 1)
                v.wait_ge(sam_sum, q + 1)
                nc.vector.tensor_scalar(at, at, vecs[:, b, WIDTH:WIDTH + 1], None, ALU.add).then_inc(sam_acc, 1)

            def variance(which):
                nc.vector.tensor_scalar(lr[:, which, 0:TILES], mv[:, which, :, 1], 0.0, None, ALU.max).then_inc(var_done, 1)
                v.wait_ge(sd_done, which + 1)
                link(nc.vector.reciprocal(lr[:, which, 0:TILES], lr[:, which, 0:TILES]))

            v.wait_ge(const, N_CONST)
            v.wait_ge(setup_sb, 1 + 2 * CB)
            MID = WIDTH // 2 + 1
            glu(0)
            first_tap(0)
            taps(0, 1, MID)
            glu(1)
            taps(0, MID, WIDTH)
            glu(2)
            first_tap(2)
            taps(2, 1, MID)
            glu(3)
            taps(2, MID, WIDTH)
            v.wait_ge(slots_clear, 16)
            first_tap(3)
            taps(3, 1, FIRST_TAPS)
            v.wait_ge(v_gelu, 2 * TILES)
            for t in range(TILES):
                r = rows(t)
                link(nc.vector.bn_stats(st[0:r, 0, t, 0:6], V[0:r, t, :]))
                link(nc.vector.bn_aggr(mv[0:r, 0, t, :], st[0:r, 0, t, 0:6]))
            variance(0)
            for t in range(TILES):
                r = rows(t)
                nc.vector.tensor_scalar(V[0:r, t, :], V[0:r, t, :], mv[0:r, 0, t, 0:1], lr[0:r, 0, t:t + 1],
                                        ALU.subtract, ALU.mult).then_inc(v_norm, 1)
            parts = CB * DEC_BATCH // SEQS
            for q in range(parts):
                left = WIDTH - FIRST_TAPS
                taps(3, FIRST_TAPS + left * q // parts, FIRST_TAPS + left * (q + 1) // parts)
                sample_sum(q)
            for t in range(TILES):
                r = rows(t)
                v.wait_ge(ct_ps, t + 1)
                link(nc.vector.bn_stats(st[0:r, 1, t, 0:6], bank[2 + t][0:r, :]))
                link(nc.vector.bn_aggr(mv[0:r, 1, t, :], st[0:r, 1, t, 0:6]))
            variance(1)
            v.wait_ge(u_gelu, CB)
            for t in range(TILES):
                r = rows(t)
                v.wait_ge(mix_ps, t + 1)
                if t >= 2:
                    v.wait_ge(yb_lo, t - 1)
                    v.wait_ge(yb_hi, t - 1)
                yb = two[:, (t % 2) * C:(t % 2 + 1) * C].rearrange("p (b n) -> p b n", b=CB)[:, :, 0:r]
                nc.vector.tensor_tensor(yb, bank[t % 2].rearrange("p (b n) -> p b n", b=CB)[:, :, 0:r],
                                        U[:, :, t * P:t * P + r], ALU.mult).then_inc(yb_mul, 1)
                v.wait_ge(yb_hi, t + 1)
                nc.vector.tensor_tensor(alo[:, CB:, t * P:t * P + r], yb, ahi[:, CB:, t * P:t * P + r].bitcast(F32),
                                        ALU.subtract).then_inc(yb_lo, 1)
            for t in range(TILES):
                r = rows(t)
                if t >= 2:
                    v.wait_ge(cc_ps, t - 1)
                nc.vector.tensor_scalar(two[0:r, D + (t % 2) * C:D + (t % 2 + 1) * C], bank[2 + t][0:r, :],
                                        mv[0:r, 1, t, 0:1], lr[0:r, 1, t:t + 1], ALU.subtract, ALU.mult)\
                    .then_inc(ct_norm, 1)
            for t in range(TILES):
                r = rows(t)
                v.wait_ge(ya_hi, t + 1)
                nc.vector.tensor_tensor(alo[:, 0:CB, t * P:t * P + r],
                                        wide[:, (t % 2) * C:(t % 2 + 1) * C].rearrange("p (b n) -> p b n", b=CB)[:, :, 0:r],
                                        ahi[:, 0:CB, t * P:t * P + r].bitcast(F32), ALU.subtract).then_inc(ya_lo, 1)

            def ffn_norm(t):
                inverse_root(FFN, t)
                v.wait_ge(gain_in, 32)
                if t >= 2:
                    v.wait_ge(normed_out[t % 2], 16 * (t // 2))
                    v.wait_ge(rt_ps, t - 1)
                apply_norm(t, FFN, two[:, (t % 2) * D:(t % 2 + 1) * D]).then_inc(norm_done, 1)

            v.wait_ge(x_again, 16 * TILES)
            for q in range(TILES * D // UC):
                i, t = divmod(q, TILES)
                at = H[0:rows(t), t, i * UC:(i + 1) * UC]
                v.wait_ge(o_ps, q + 1)
                nc.vector.tensor_tensor(at, bank[3 + q % 3][0:rows(t), 0:UC], at, ALU.add).then_inc(o_add, 1)
                if q > 3 * TILES:
                    ffn_norm(q - 3 * TILES - 1)
            for t in range(TILES):
                v.wait_ge(pt_hi, t + 1)
                nc.vector.tensor_tensor(plo[:, :, t * P:t * P + rows(t)],
                                        bank[4 + t % 2][:, 0:2 * P].rearrange("p (c n) -> p c n", c=2)[:, :, 0:rows(t)],
                                        phi[:, :, t * P:t * P + rows(t)].bitcast(F32), ALU.subtract).then_inc(pt_lo, 1)
            ffn_norm(TILES - 1)

            v.wait_ge(small_in, 16 * 5)
            v.wait_ge(r_ps, TILES)
            NL = GROUPS + EXPERTS
            logits = bank[2][:, 0:TILES * NL].rearrange("p (t n) -> p t n", t=TILES)
            full = TILES - 1
            link(nc.vector.tensor_tensor(lg[:, 0:full, :], logits[:, 0:full, :],
                                         rb[:, :].unsqueeze(1).to_broadcast([P, full, NL]), ALU.add))
            link(nc.vector.tensor_tensor(lg[0:SAMPLE, full, :], logits[0:SAMPLE, full, :], rb[0:SAMPLE, :], ALU.add))
            v.sem_inc(lg_sb, 1)
            gl = lg[:, :, 0:GROUPS]
            el = lg[:, :, GROUPS:].rearrange("p t (g k) -> p t g k", g=GROUPS)

            def over(x, n=GROUPS):
                return x.unsqueeze(2).to_broadcast([P, TILES, n])

            def first_max(values, top, hot, tmp):
                link(nc.vector.tensor_reduce(top, values, AX_X, ALU.max))
                link(nc.vector.tensor_tensor(tmp, values, over(top), ALU.is_equal))
                link(nc.vector.tensor_tensor(tmp, tmp, rev[:, :].unsqueeze(1).to_broadcast([P, TILES, GROUPS]), ALU.mult))
                link(nc.vector.tensor_reduce(r1[:, 15, :], tmp, AX_X, ALU.max))
                link(nc.vector.tensor_tensor(hot, tmp, over(r1[:, 15, :]), ALU.is_equal))

            gmax, gsum, diff, gw, m1, m2, den, w1, w2 = (r1[:, i, :] for i in range(9))
            diff = r1[:, 2, :]
            egl, hot_g, elg, hot1, hot2, tmp4, rest = (r4[:, i, :, :] for i in range(7))
            M1, M2, M, earlier, spare, spare2 = (r16[:, i, :, :] for i in range(6))

            def by_group(x):
                return x.rearrange("p t (g k) -> p t g k", g=GROUPS)

            first_max(gl, gmax, hot_g, tmp4)
            nc.vector.tensor_tensor(egl, gl, over(gmax), ALU.subtract).then_inc(arg_done, 1)
            hot_gk = hot_g.unsqueeze(3).to_broadcast([P, TILES, GROUPS, PER])
            link(nc.vector.tensor_tensor(by_group(spare), el, hot_gk, ALU.mult))
            link(nc.vector.tensor_reduce(elg, spare.rearrange("p t (g k) -> p t k g", g=GROUPS), AX_X, ALU.add))
            first_max(elg, m1, hot1, tmp4)
            link(nc.vector.scalar_tensor_tensor(out=rest, in0=hot1, scalar=-BIG, in1=elg, op0=ALU.mult, op1=ALU.add))
            first_max(rest, m2, hot2, tmp4)
            nc.vector.tensor_tensor(diff, m2, m1, ALU.subtract).then_inc(arg_done, 1)
            for hot, m in ((hot1, M1), (hot2, M2)):
                link(nc.vector.tensor_tensor(by_group(m), hot_gk,
                                             hot.unsqueeze(2).to_broadcast([P, TILES, GROUPS, PER]), ALU.mult))
            link(nc.vector.tensor_tensor(M, M1, M2, ALU.add))
            link(nc.vector.memset(M[SAMPLE:, full, :], 0.0))
            link(nc.vector.memset(earlier[:, 0, :], 0.0))
            for t in range(1, TILES):
                link(nc.vector.tensor_tensor(earlier[:, t, :], earlier[:, t - 1, :], M[:, t - 1, :], ALU.add))
            nc.vector.tensor_tensor(spare2[:, 0, :], earlier[:, full, :], M[:, full, :], ALU.add).then_inc(onehot, 1)
            v.wait_ge(exp_done, 2)
            link(nc.vector.tensor_reduce(gsum, egl, AX_X, ALU.add))
            link(nc.vector.reciprocal(gw, gsum))
            link(nc.vector.tensor_scalar(den, diff, 1.0, None, ALU.add))
            link(nc.vector.reciprocal(den, den))
            link(nc.vector.tensor_tensor(w1, den, gw, ALU.mult))
            link(nc.vector.tensor_tensor(w2, w1, diff, ALU.mult))
            v.wait_ge(rank_ps, 1)
            link(nc.vector.tensor_tensor(spare, bank[5][:, 0:TILES * EXPERTS].rearrange("p (t e) -> p t e", t=TILES),
                                         base[:, :].unsqueeze(1).to_broadcast([P, TILES, EXPERTS]), ALU.add))
            for k, m in enumerate((M1, M2)):
                link(nc.vector.tensor_tensor(m, m, spare, ALU.mult))
                link(nc.vector.tensor_reduce(r1[:, 9 + k, :], m, AX_X, ALU.add))
                nc.vector.tensor_copy(pos[:, :, k], r1[:, 9 + k, :]).then_inc(dve, 1)
                own[0] += 1
            v.wait_ge(dve, own[0])
            v.sem_inc(slot_at, 1)
            counts = bank[5][0:1, P:P + EXPERTS]
            for t in range(4):
                link(nc.vector.tensor_scalar(wl[:, 0, t * EXPERTS:(t + 1) * EXPERTS], counts, float(P * (t + 1)), None,
                                             ALU.is_gt))
            link(nc.vector.tensor_tensor_scan(wl[:, 1, :], wl[:, 0, :], wl[:, 2, :], 0.0, ALU.add, ALU.add))
            for j in range(OVERFLOW_MAX):
                link(nc.vector.scalar_tensor_tensor(out=wl8[:, 0, j, :], in0=wl[:, 1, :], scalar=float(j + 1),
                                                    in1=wl[:, 0, :], op0=ALU.is_equal, op1=ALU.mult))
            for q in range(2):
                link(nc.vector.tensor_tensor(wl8[:, 1, :, :], wl8[:, 0, :, :],
                                             codes[:, q, :].unsqueeze(1).to_broadcast([1, OVERFLOW_MAX, 4 * EXPERTS]),
                                             ALU.mult))
                link(nc.vector.tensor_reduce(jobs[:, q * OVERFLOW_MAX:(q + 1) * OVERFLOW_MAX], wl8[:, 1, :, :], AX_X, ALU.add))
            link(nc.vector.tensor_copy(jobs[:, 2 * OVERFLOW_MAX:], wl[:, 1, 4 * EXPERTS - 1:]))
            nc.vector.tensor_copy(jobs_i[:, :], jobs[:, :]).then_inc(jobs_done, 1)

            def split_low(n, d=0):
                v.wait_ge(hi_done, n + 1 + 6 * d)
                wait_used(v, n - SPLIT, d)
                s = slice(0, UNIT - LOW_POOL)
                nc.vector.tensor_tensor(lo[:, n % SPLIT, s], raw[:, n % RAW, s], hi[:, n % SPLIT, s].bitcast(F32),
                                        ALU.subtract).then_inc(lo_dve, 1)

            def hidden(e0, d=0):
                v.wait_ge(silu_done, e0 + 1 + d)
                wait_used(v, N_MOE + 3 if e0 == 0 else step_unit(e0, 3), d)
                if e0 > 0:
                    v.wait_ge(t_ps, e0 + d)
                nc.vector.tensor_tensor(hid, bank[1], silu, ALU.mult).then_inc(hid_done, 1)

            def gather_low(e0, d=0):
                v.wait_ge(g_hi, e0 + 1 + d)
                nc.vector.tensor_tensor(xlo, pair[1][:, :].rearrange("p (c n) -> p c n", c=DC), xhi.bitcast(F32),
                                        ALU.subtract).then_inc(g_lo, 1)

            def hidden_low(e0, d=0):
                v.wait_ge(t_hi, e0 + 1 + d)
                nc.vector.tensor_tensor(tlo, bank[4].rearrange("p (c n) -> p c n", c=CB), thi.bitcast(F32),
                                        ALU.subtract).then_inc(t_lo, 1)

            def result(n, e0, d=0):
                wait_used(v, n, d)
                if e0 > 0:
                    v.wait_ge(scattered, 16 * (e0 + d))
                nc.vector.tensor_copy(res[:, C:], bank[7]).then_inc(res_dve, 1)

            def step(e0, d=0):
                if e0 == 0:
                    split_low(N_MOE + 2)
                    split_low(N_MOE + 3)
                    hidden(0)
                    gather_low(1)
                    split_low(N_STEP)
                    split_low(N_STEP + 1)
                    hidden_low(0)
                    return
                for k in range(2, 6):
                    split_low(step_unit(e0, k), d)
                hidden(e0, d)
                if e0 < EXPERTS - 1:
                    gather_low(e0 + 1, d)
                split_low(step_unit(e0, 6), d)
                split_low(step_unit(e0, 7), d)
                hidden_low(e0, d)
                result(step_unit(e0, 5), e0 - 1, d)

            split_low(N_MOE)
            split_low(N_MOE + 1)
            gather_low(0)
            step(0)
            step(1)
            with v.Fori(0, EXPERTS - 3) as d:
                step(2, d)
            step(EXPERTS - 1)
            result(N_GATE - 1, EXPERTS - 1)

            v.wait_ge(jobs_done, 1)
            jobs_n = v.value_load(jobs_i[0:1, 2 * OVERFLOW_MAX:], min_val=0, max_val=OVERFLOW_MAX)
            with v.If(jobs_n > 0):
                with v.Fori(0, jobs_n) as j:
                    v.wait_ge(v_silu, j + 1)
                    nc.vector.tensor_tensor(hid, bank[1], silu, ALU.mult).then_inc(v_hid, 1)

            for n in range(N_GATE, N_GATE + SPLIT):
                split_low(n)
            def gated(q, i, t):
                r = rows(t)
                s = wide[0:r, (q % 4) * UC:(q % 4 + 1) * UC]
                at = H[0:r, t, i * UC:(i + 1) * UC]
                v.wait_ge(s_sig, q + 1)
                nc.vector.tensor_tensor(s, s, PP[0:r, t, i * UC:(i + 1) * UC], ALU.mult).then_inc(s_mul, 1)
                v.wait_ge(s_mul, q + 1)
                nc.vector.tensor_tensor(at, at, s, ALU.add).then_inc(s_add, 1)

            for t in range(TILES + 1):
                if t < TILES:
                    r = rows(t)
                    v.wait_ge(pair_in[t % 2], 16 * (t // 2 + 1))
                    nc.vector.scalar_tensor_tensor(out=H[0:r, t, :], in0=raw[0:r, PAIR_SLOTS[t % 2], 0:D],
                                                   scalar=w1[0:r, t:t + 1], in1=H[0:r, t, :], op0=ALU.mult,
                                                   op1=ALU.add).then_inc(pair_one, 1)
                if t >= 1:
                    inverse_root(GATE, t - 1)
                    v.wait_ge(gain_in, 48)
                    if t >= 3:
                        v.wait_ge(xt_ps, TILES + t - 2)
                    apply_norm(t - 1, GATE, two[:, (t - 1) % 2 * D:((t - 1) % 2 + 1) * D]).then_inc(norm_done, 1)
                if t >= 2:
                    normed_low(t - 2, GATE)
                if t >= 3:
                    for i in range(SPLIT):
                        gated(SPLIT * (t - 3) + i, i, t - 3)
            normed_low(TILES - 1, GATE)

            def final_norm(t):
                inverse_root(FINAL, t)
                v.wait_ge(gain_in, 64)
                if t >= 2:
                    v.wait_ge(y_out[t % 2], 16 * (t // 2))
                apply_norm(t, FINAL, two[:, (t % 2) * D:(t % 2 + 1) * D]).then_inc(y_sb, 1)

            for q, (i, t) in list(enumerate(GATE_ORDER))[SPLIT * (TILES - 2):]:
                if q == 3 * TILES - 1:
                    split_low(N_GATE + SPLIT)
                if q == 4 * TILES - 1:
                    final_norm(0)
                    final_norm(1)
                gated(q, i, t)
            for t in range(2, TILES):
                final_norm(t)

        @block.tensor
        def _(pe):
            mm, tr = nc.tensor.matmul, nc.tensor.transpose

            def wait_unit(n, d=0):
                pe.wait_ge(hi_done, n + 1 + 6 * d)
                pe.wait_ge(lo_pool, n + 1 + 6 * d)
                if n >= N_MOE:
                    pe.wait_ge(lo_dve, n - N_MOE + 1 + 6 * d)

            def split_product(out_, x_hi, x_lo, w_hi, w_lo, start, stop):
                mm(out_, x_hi, w_hi, start=start, stop=False)
                mm(out_, x_hi, w_lo, start=False, stop=False)
                return mm(out_, x_lo, w_hi, start=False, stop=stop)

            def unit(n, c):
                return (s[:, n % SPLIT, :].rearrange("p (c n) -> p c n", c=c) for s in (hi, lo))

            def transpose_rows(src, r, to):
                for c in range(DC):
                    ins = tr(to[:, c * P:c * P + r], src[0:r, c * P:(c + 1) * P], ident[0:r, 0:r])
                return ins

            def normed_tiles(w, src):
                for t in range(TILES):
                    first = 0 if w == MIX else TILES
                    pe.wait_ge(norm_done, w * TILES + t + 1)
                    if t >= 2:
                        pe.wait_ge(xt_lo, first + t - 1)
                    transpose_rows(src(t), rows(t), pair[t % 2]).then_inc(xt_ps, 1)

            pe.wait_ge(const, 2)
            normed_tiles(MIX, lambda t: H[:, t, :])
            pe.wait_ge(rows_in, 16 * 6)
            for b in range(CB):
                ins = tr(bank[4][:, b * P:b * P + NV], vrow[0:NV, b * P:(b + 1) * P], ident[0:NV, 0:NV])
            ins.then_inc(setup_ps, 1)
            for i in range(2):
                for b in range(CB):
                    ins = tr(bank[5 + i][:, b * P:b * P + SROWS], stn[0:SROWS, i, b * P:(b + 1) * P],
                             ident[0:SROWS, 0:SROWS])
                ins.then_inc(setup_ps, 1)

            def channel_block(n, half, banks, bank_sem):
                w_hi, w_lo = unit(n, DC)
                cols = slice(half * P, (half + 1) * P)
                outs = [banks[:, s * 512:s * 512 + HALF] for s in range(2)]
                for c in range(DC):
                    for w, x, last in ((w_hi, ahi, False), (w_hi, alo, False), (w_lo, ahi, True)):
                        for s in range(2):
                            ins = mm(outs[s], w[:, c, cols], x[:, c, s * HALF:(s + 1) * HALF],
                                     start=(c == 0 and w is w_hi and x is ahi), stop=(c == DC - 1 and last))
                ins.then_inc(bank_sem, 1)

            pe.wait_ge(xt_lo, TILES)
            pe.wait_ge(setup_sb, 1 + 2 * CB)
            for b in range(CB):
                n = 2 * (b // 2)
                if b % 2 == 0:
                    wait_unit(n)
                if b >= 2:
                    pe.wait_ge(glu_done, 3 * (b - 1))
                channel_block(n, b % 2, pair[2 * (b % 2)], z_ps)
                if b % 2 == 0:
                    wait_unit(n + 1)
                channel_block(n + 1, b % 2, pair[2 * (b % 2) + 1], z_ps)

            def token_rows(q, n, to, i_sem, x_hi=ahi, x_lo=alo):
                t = q % TILES
                r = rows(t)
                w_hi, w_lo = unit(n, DC)
                for c in range(DC):
                    ins = split_product(to[0:r, 0:UC], x_hi[:, c, t * P:t * P + r], x_lo[:, c, t * P:t * P + r],
                                        w_hi[:, c, :], w_lo[:, c, :], c == 0, c == DC - 1)
                return ins.then_inc(i_sem, 1)

            pe.wait_ge(glu_done, 9)
            for q in range(2 * TILES):
                n = 4 + q // TILES
                if q % TILES == 0:
                    wait_unit(n)
                if q >= 4:
                    pe.wait_ge(v_gelu, q - 3)
                token_rows(q, n, bank[q % 4], v_ps)
            pe.wait_ge(glu_done, 12)
            for b in range(CB):
                n = 6 + b // 2
                if b % 2 == 0:
                    wait_unit(n)
                if b >= 2:
                    pe.wait_ge(u_gelu, b - 1)
                channel_block(n, b % 2, pair[2 + b % 2], u_ps)
            pe.wait_ge(masked, 2)
            pe.wait_ge(v_gelu, 2 * TILES)
            for i in range(HEADS):
                ins = tr(pair[0][:, i * P:(i + 1) * P], wsn[:, i, :], ident[:, :])
            ins.then_inc(setup_ps, 1)
            for i in range(HEADS):
                ins = tr(bank[2][0:SAMPLE, i * SAMPLE:(i + 1) * SAMPLE], wssn[0:SAMPLE, i, :], ident[0:SAMPLE, 0:SAMPLE])
            ins.then_inc(setup_ps, 1)
            pe.wait_ge(setup_sb, 3 + 2 * CB)
            pe.wait_ge(small_in, 16 * 5)
            for t in range(TILES):
                r = rows(t)
                if t == 2:
                    pe.wait_ge(acc, WIDTH * len(DVE_BLOCKS))
                    pe.wait_ge(tap_add, WIDTH - 1)
                    pe.wait_ge(sam_acc, CB * DEC_BATCH // SEQS)
                    pe.wait_ge(u_gelu, CB)
                    for u in range(TILES):
                        for b in range(CB):
                            ins = tr(bank[2 + u][0:rows(u), b * P:(b + 1) * P], A[:, b, u * P:u * P + rows(u)], ident[:, :])
                        ins.then_inc(ct_ps, 1)
                pe.wait_ge(v_ready, t + 1)
                if t >= 2:
                    pe.wait_ge(yb_mul, t - 1)
                for i in range(HEADS):
                    at = (i % 2) * HD
                    to = bank[t % 2][at:at + HD, (i // 2) * P:(i // 2) * P + r]
                    w = WS[0:r, i, 0:r] if t < TILES - 1 else WSS[0:r, i, :]
                    mm(to, V[0:r, t, i * HD:(i + 1) * HD], w, start=True, stop=False)
                    if t < TILES - 1:
                        ins = mm(to, ones[BS:BS + 1, 0:HD], bs[:, i * P:(i + 1) * P], start=False, stop=True)
                    else:
                        b_row = bs[:, i * P:i * P + DEC_SEQ].unsqueeze(1).to_broadcast([1, DEC_BATCH, DEC_SEQ])
                        ins = mm(to, ones[BS:BS + 1, 0:HD], b_row, start=False, stop=True)
                ins.then_inc(mix_ps, 1)
            pe.wait_ge(yb_mul, TILES)
            for t in range(TILES):
                r = rows(t)
                pe.wait_ge(ct_norm, t + 1)
                if t >= 2:
                    pe.wait_ge(ya_silu, CB * (t - 1))
                for b in range(CB):
                    at = D + (t % 2) * C + b * P
                    ins = tr(bank[(7, 1)[t % 2]][:, b * P:b * P + r], two[0:r, at:at + P], ident[0:r, 0:r])
                ins.then_inc(cc_ps, 1)
            pe.wait_ge(fresh_done, 1)
            for b in range(CB):
                ins = tr(bank[6][0:HIST, b * P:(b + 1) * P], G[:, b, GP - HIST:GP], ident[:, :])
            ins.then_inc(state_ps, 1)
            for b in range(CB):
                ins = tr(bank[0][0:SAMPLE, b * P:(b + 1) * P], fresh[:, b, :], ident[:, :])
            ins.then_inc(state_ps, 1)
            def router(t):
                r = rows(t)
                NL = GROUPS + EXPERTS
                pe.wait_ge(norm_done, TILES + t + 1)
                if t >= 2:
                    pe.wait_ge(rt_sb, t - 1)
                transpose_rows(two[:, (t % 2) * D:(t % 2 + 1) * D], r, pair[(0, 3)[t % 2]]).then_inc(rt_ps, 1)
                pe.wait_ge(rt_sb, t + 1)
                for c in range(DC):
                    ins = mm(bank[2][0:r, t * NL:(t + 1) * NL], wide[:, c * P:c * P + r], wr[:, c, :],
                             start=(c == 0), stop=(c == DC - 1))
                ins.then_inc(r_ps, 1)

            pe.wait_ge(yb_lo, TILES)
            for q in range(TILES * D // UC):
                n = N_OUT + q // TILES
                if q % TILES == 0:
                    wait_unit(n)
                if q < TILES:
                    pe.wait_ge(ya_lo, q + 1)
                if q >= 3:
                    pe.wait_ge(o_add, q - 2)
                if q == 3 * TILES:
                    pe.wait_ge(state_sb, 2)
                token_rows(q, n, bank[3 + q % 3], o_ps)
                if q >= 3 * TILES + 2:
                    router(q - 3 * TILES - 2)
            pe.wait_ge(p_in, 16 * TILES)
            pe.wait_ge(o_add, TILES * D // UC)
            for t in range(TILES):
                r = rows(t)
                if t >= 2:
                    pe.wait_ge(pt_lo, t - 1)
                for c in range(2):
                    ins = tr(bank[4 + t % 2][:, c * P:c * P + r], PN[0:r, t, c * P:(c + 1) * P], ident[0:r, 0:r])
                ins.then_inc(pt_ps, 1)
            router(TILES - 2)
            router(TILES - 1)
            pe.wait_ge(pt_lo, TILES)

            def embedding(t):
                r = rows(t)
                w_hi, w_lo = unit(N_PROJ, 2)
                if t >= 2:
                    pe.wait_ge(pp_sb, t - 1)
                for half in range(2):
                    for c in range(2):
                        s = slice(half * C, (half + 1) * C)
                        ins = split_product(pair[(0, 3)[t % 2]][0:r, s], phi[:, c, t * P:t * P + r],
                                            plo[:, c, t * P:t * P + r], w_hi[:, c, s], w_lo[:, c, s], c == 0, c == 1)
                return ins.then_inc(pp_ps, 1)

            wait_unit(N_PROJ)
            pe.wait_ge(rt_sb, TILES)
            embedding(0)
            embedding(1)
            pe.wait_ge(onehot, 1)
            M, earlier = r16[:, 2, :, :], r16[:, 3, :, :]
            flat = "p t e -> p (t e)"
            mm(bank[5][:, 0:TILES * EXPERTS], before[:, :], M.rearrange(flat), start=True, stop=False)
            mm(bank[5][:, 0:TILES * EXPERTS], ones[:, :], earlier.rearrange(flat), start=False, stop=True)
            mm(bank[5][:, P:P + EXPERTS], ones[:, :], r16[:, 5, 0, :], start=True, stop=True).then_inc(rank_ps, 1)
            for t in range(2, TILES):
                embedding(t)

            def transpose_gathered(e0, d=0):
                pe.wait_ge(gathered, 16 * (e0 + 1) + 16 * d)
                if e0 > 0:
                    pe.wait_ge(g_lo, e0 + d)
                transpose_rows(xg, P, pair[1]).then_inc(g_ps, 1)

            def gate_up(n, e0, d=0):
                pe.wait_ge(g_lo, e0 + 1 + d)
                if e0 > 0:
                    pe.wait_ge(hid_done, e0 + d)
                for k in range(4):
                    wait_unit(n + k, d)
                    w_hi, w_lo = unit(n + k, DC // 2)
                    for c in range(DC // 2):
                        at = (k % 2) * (DC // 2) + c
                        ins = split_product(bank[k // 2], xhi[:, at, :], xlo[:, at, :], w_hi[:, c, :], w_lo[:, c, :],
                                            at == 0, at == DC - 1)
                    ins.then_inc(pe_unit, 1)

            def transpose_hidden(e0, d=0):
                pe.wait_ge(hid_done, e0 + 1 + d)
                if e0 > 0:
                    pe.wait_ge(t_lo, e0 + d)
                for c in range(CB):
                    ins = tr(bank[4][:, c * P:(c + 1) * P], hid[:, c * P:(c + 1) * P], ident[:, :])
                ins.then_inc(t_ps, 1)

            def down(n, e0, d=0):
                pe.wait_ge(t_lo, e0 + 1 + d)
                if e0 > 0:
                    pe.wait_ge(res_act, e0 + d)
                    pe.wait_ge(res_dve, e0 + d)
                for k in range(2):
                    wait_unit(n + k, d)
                    w_hi, w_lo = unit(n + k, 2)
                    for c in range(2):
                        at = 2 * k + c
                        for half in range(2):
                            s = slice(half * C, (half + 1) * C)
                            ins = split_product(bank[6 + half], thi[:, at, :], tlo[:, at, :], w_hi[:, c, s], w_lo[:, c, s],
                                                at == 0, at == CB - 1)
                    ins.then_inc(pe_unit, 1)

            def step(e0, d=0):
                gate_up(N_MOE if e0 == 0 else step_unit(e0, 0), e0, d)
                if e0 < EXPERTS - 1:
                    transpose_gathered(e0 + 1, d)
                if e0 > 0:
                    down(step_unit(e0, 4), e0 - 1, d)
                transpose_hidden(e0, d)

            pe.wait_ge(lg_sb, 1)
            pe.wait_ge(pp_sb, TILES)
            transpose_gathered(0)
            step(0)
            step(1)
            with pe.Fori(0, EXPERTS - 3) as d:
                step(2, d)
            step(EXPERTS - 1)
            down(N_GATE - 2, EXPERTS - 1)

            pe.wait_ge(jobs_done, 1)
            jobs_n = pe.value_load(jobs_i[0:1, 2 * OVERFLOW_MAX:], min_val=0, max_val=OVERFLOW_MAX)

            def weights(i, c):
                n, per, width = N_GATE - RAW + 2 * i, (CB if i == 2 else DC) // 2, D if i == 2 else DE
                return raw[:, (n + c // per) % RAW, c % per * width:(c % per + 1) * width]

            with pe.If(jobs_n > 0):
                pe.wait_ge(t_lo, EXPERTS)
                pe.wait_ge(res_act, EXPERTS)
                pe.wait_ge(res_dve, EXPERTS)
                with pe.Fori(0, jobs_n) as j:
                    pe.wait_ge(v_in, 16 * j + 16)
                    transpose_rows(xg, P, pair[1]).then_inc(v_gps, 1)
                    pe.wait_ge(v_gsb, j + 1)
                    for i in range(2):
                        pe.wait_ge(v_w[i], 32 * j + 32)
                        for c in range(DC):
                            ins = mm(bank[i], wide[:, c * P:(c + 1) * P], weights(i, c),
                                     start=(c == 0), stop=(c == DC - 1))
                    ins.then_inc(v_gu, 1)
                    pe.wait_ge(v_hid, j + 1)
                    for c in range(CB):
                        ins = tr(bank[4][:, c * P:(c + 1) * P], hid[:, c * P:(c + 1) * P], ident[:, :])
                    ins.then_inc(v_tps, 1)
                    pe.wait_ge(v_tsb, j + 1)
                    pe.wait_ge(v_w[2], 32 * j + 32)
                    for c in range(CB):
                        for half in range(2):
                            ins = mm(bank[6 + half], wide[:, c * P:(c + 1) * P], weights(2, c)[:, half * C:(half + 1) * C],
                                     start=(c == 0), stop=(c == CB - 1))
                    ins.then_inc(v_dps, 1)

            def gate_rows(t):
                if t >= 2:
                    pe.wait_ge(xt_lo, TILES + t - 1)
                pe.wait_ge(norm_done, 2 * TILES + t + 1)
                transpose_rows(two[:, (t % 2) * D:(t % 2 + 1) * D], rows(t), pair[t % 2]).then_inc(xt_ps, 1)

            gate_rows(0)
            for q, (i, t) in enumerate(GATE_ORDER):
                if i == SPLIT - 1 and t + 1 < TILES:
                    gate_rows(t + 1)
                if t == 0:
                    wait_unit(N_GATE + i)
                if i == 0:
                    pe.wait_ge(xt_lo, TILES + t + 1)
                if q >= 4:
                    pe.wait_ge(s_sig, q - 3)
                token_rows(t, N_GATE + i, bank[4 + q % 4], s_ps)


_INS = ["x_prompt", "x_sample", "p_prompt", "p_sample", "state_conv", "norm_mix_g", "w_in", "conv_w", "conv_b",
        "conv_ln_g", "conv_ln_b", "gmlp_ln_g", "gmlp_ln_b", "w_s", "b_s", "w_out", "norm_ffn_g", "w_router_group",
        "b_router_group", "w_router_expert", "b_router_expert", "w_exp_gate", "w_exp_up", "w_exp_down", "norm_ple_g",
        "w_ple_gate", "w_ple_proj", "norm_final_g"]
_OUTS = [("y_prompt", (1, SEQ, D)), ("y_sample", (DEC_BATCH, DEC_SEQ, D)), ("state_conv_prompt", (1, 1, HIST, C)),
         ("state_conv_sample", (1, DEC_BATCH, HIST, C)), ("state_gmlp_v_sample", (1, DEC_BATCH, DEC_SEQ, C))]


def kernel(**inputs):
    import numpy as _np
    import concourse.bacc as _bacc
    from concourse import mybir as _mybir
    from concourse.bass_utils import run_bass_kernel_spmd as _run

    nc = _bacc.Bacc("TRN2", target_bir_lowering=False, num_devices=1)
    arrays, ins, outs = {}, {}, {}
    for name in _INS:
        x = _np.ascontiguousarray(inputs[name])
        arrays[f"in_{name}"] = x
        ins[name] = nc.dram_tensor(f"in_{name}", x.shape, _mybir.dt.from_np(x.dtype), kind="ExternalInput").ap()
    for name, shape in _OUTS:
        outs[name] = nc.dram_tensor(f"out_{name}", shape, _mybir.dt.float32, kind="ExternalOutput").ap()
    hybrid_layer(nc, ins, outs)
    r = _run(nc, [arrays], core_ids=[0])
    return tuple(r.results[0][f"out_{name}"] for name, _ in _OUTS)
```
